# Optimizing a Trainium2 kernel written in Bass

```python
import math
import jax, jax.numpy as jnp
from jax import lax
import numpy as np

D_MODEL = 1024
BATCH = 1
SEQ = 512
DEPTH = 2

N_MIXERS = 2
N_SGU_LAYERS = (DEPTH + 1) // 2
N_SWA_LAYERS = DEPTH // 2

CHUNK = 128
SGU_WIDTH = 2 * D_MODEL
SGU_GROUPS = 16
SGU_GROUP_DIM = SGU_WIDTH // SGU_GROUPS

HEAD_DIM = 64
N_HEADS = D_MODEL // HEAD_DIM
N_KV_HEADS = 4
KV_GROUP = N_HEADS // N_KV_HEADS
WINDOW = 128
BLOCK = WINDOW

REL_BUCKETS = 32
REL_MAX_DIST = 128

D_FF = 2816
CONV_WIDTH = 3

EPS = 1e-6

kernel_name = "hybrid_sgu_swa_convffn"

def rms_norm(x, gain):
    xf = x.astype(jnp.float32)
    y = xf * lax.rsqrt(jnp.mean(xf * xf, axis=-1, keepdims=True) + EPS)
    return (y * gain.astype(jnp.float32)).astype(x.dtype)

def _rel_buckets():
    q = np.arange(BLOCK)[:, None] + BLOCK
    k = np.arange(2 * BLOCK)[None, :]
    dist = q - k
    n = np.maximum(dist, 0)
    max_exact = REL_BUCKETS // 2
    large = max_exact + (np.log(np.maximum(n, 1).astype(np.float32) / max_exact)
                         / math.log(REL_MAX_DIST / max_exact)
                         * (REL_BUCKETS - max_exact)).astype(np.int32)
    large = np.minimum(large, REL_BUCKETS - 1)
    bucket = np.where(n < max_exact, n, large).astype(np.int32)
    return dist, bucket

def sgu_mixer(h, w_in, v_gain, w_s, b_s, w_out):
    B, S, _ = h.shape
    nc = S // CHUNK
    z = jax.nn.gelu(h @ w_in, approximate=False)
    u, v = jnp.split(z, 2, axis=-1)
    v = rms_norm(v, v_gain).reshape(B, nc, CHUNK, SGU_GROUPS, SGU_GROUP_DIM)
    w_causal = jnp.tril(w_s)
    s = jnp.einsum('gts,bcsgd->bctgd', w_causal, v) + b_s.T[:, :, None]
    return (u * s.reshape(B, S, SGU_WIDTH)) @ w_out

def swa_mixer(h, w_qkv, q_gain, k_gain, sinks, w_o, rel_bias):
    B, S, _ = h.shape
    nb = S // BLOCK
    qkv = h @ w_qkv
    q, k, v = jnp.split(qkv, [N_HEADS * HEAD_DIM, (N_HEADS + N_KV_HEADS) * HEAD_DIM], axis=-1)
    q = rms_norm(q.reshape(B, S, N_HEADS, HEAD_DIM), q_gain)
    k = rms_norm(k.reshape(B, S, N_KV_HEADS, HEAD_DIM), k_gain)
    v = v.reshape(B, S, N_KV_HEADS, HEAD_DIM)
    q = q.reshape(B, nb, BLOCK, N_KV_HEADS, KV_GROUP, HEAD_DIM)

    def band(t):
        t = t.reshape(B, nb, BLOCK, N_KV_HEADS, HEAD_DIM)
        prev = jnp.pad(t, ((0, 0), (1, 0), (0, 0), (0, 0), (0, 0)))[:, :-1]
        return jnp.concatenate([prev, t], axis=2)

    kb, vb = band(k), band(v)
    scores = jnp.einsum('bnqhgd,bnkhd->bnhgqk', q, kb).astype(jnp.float32) * (HEAD_DIM ** -0.5)

    dist, bucket = _rel_buckets()
    bias = rel_bias.astype(jnp.float32)[bucket]
    bias = jnp.transpose(bias, (2, 0, 1)).reshape(N_KV_HEADS, KV_GROUP, BLOCK, 2 * BLOCK)
    scores = scores + bias

    blk = np.arange(nb)[:, None, None]
    kk = np.arange(2 * BLOCK)[None, None, :]
    valid = ((dist >= 0) & (dist < WINDOW))[None] & ((blk > 0) | (kk >= BLOCK))
    scores = jnp.where(valid[None, :, None, None], scores, -jnp.inf)

    sink = sinks.astype(jnp.float32).reshape(N_KV_HEADS, KV_GROUP)[None, None, :, :, None, None]
    m = jnp.maximum(jnp.max(scores, axis=-1, keepdims=True), sink)
    p = jnp.exp(scores - m)
    denom = jnp.sum(p, axis=-1, keepdims=True) + jnp.exp(sink - m)
    p = (p / denom).astype(vb.dtype)
    o = jnp.einsum('bnhgqk,bnkhd->bnqhgd', p, vb).reshape(B, S, N_HEADS * HEAD_DIM)
    return o @ w_o

def conv_glu_ffn(h, w_up, conv_w, conv_b, w_down):
    a = h @ w_up
    C = a.shape[-1]
    c = lax.conv_general_dilated(a, conv_w[:, None, :].astype(a.dtype), window_strides=(1,),
                                 padding=[(CONV_WIDTH - 1, 0)],
                                 dimension_numbers=('NWC', 'WIO', 'NWC'),
                                 feature_group_count=C) + conv_b
    g, val = jnp.split(c, 2, axis=-1)
    return (jax.nn.silu(g) * val) @ w_down

def setup_inputs(seed: int = 0) -> dict:
    key = jax.random.key(seed)
    ks = jax.random.split(key, 20)
    f32 = jnp.float32
    nrm = lambda k, shape, scale: jax.random.normal(k, shape, f32) * scale
    return {
        "x": nrm(ks[0], (BATCH, SEQ, D_MODEL), 1.0),
        "mix_norm": 1.0 + nrm(ks[1], (DEPTH, D_MODEL), 0.05),
        "ffn_norm": 1.0 + nrm(ks[2], (DEPTH, D_MODEL), 0.05),
        "sgu_w_in": nrm(ks[3], (N_SGU_LAYERS, D_MODEL, 2 * SGU_WIDTH), D_MODEL ** -0.5),
        "sgu_v_gain": 1.0 + nrm(ks[4], (N_SGU_LAYERS, SGU_WIDTH), 0.05),
        "sgu_w_s": nrm(ks[5], (N_SGU_LAYERS, SGU_GROUPS, CHUNK, CHUNK), CHUNK ** -0.5),
        "sgu_b_s": 1.0 + nrm(ks[6], (N_SGU_LAYERS, SGU_GROUPS, CHUNK), 0.05),
        "sgu_w_out": nrm(ks[7], (N_SGU_LAYERS, SGU_WIDTH, D_MODEL), SGU_WIDTH ** -0.5),
        "attn_w_qkv": nrm(ks[8], (N_SWA_LAYERS, D_MODEL, (N_HEADS + 2 * N_KV_HEADS) * HEAD_DIM), D_MODEL ** -0.5),
        "attn_q_gain": 1.0 + nrm(ks[9], (N_SWA_LAYERS, HEAD_DIM), 0.05),
        "attn_k_gain": 1.0 + nrm(ks[10], (N_SWA_LAYERS, HEAD_DIM), 0.05),
        "attn_sinks": nrm(ks[11], (N_SWA_LAYERS, N_HEADS), 0.5),
        "attn_w_o": nrm(ks[12], (N_SWA_LAYERS, N_HEADS * HEAD_DIM, D_MODEL), (N_HEADS * HEAD_DIM) ** -0.5),
        "rel_bias": nrm(ks[13], (REL_BUCKETS, N_HEADS), 0.5),
        "ffn_w_up": nrm(ks[14], (DEPTH, D_MODEL, 2 * D_FF), D_MODEL ** -0.5),
        "ffn_conv_w": nrm(ks[15], (DEPTH, CONV_WIDTH, 2 * D_FF), CONV_WIDTH ** -0.5),
        "ffn_conv_b": nrm(ks[16], (DEPTH, 2 * D_FF), 0.02),
        "ffn_w_down": nrm(ks[17], (DEPTH, D_FF, D_MODEL), D_FF ** -0.5),
    }

def reference(x, mix_norm, ffn_norm, sgu_w_in, sgu_v_gain, sgu_w_s, sgu_b_s, sgu_w_out,
              attn_w_qkv, attn_q_gain, attn_k_gain, attn_sinks, attn_w_o, rel_bias,
              ffn_w_up, ffn_conv_w, ffn_conv_b, ffn_w_down):
    h = x
    for i in range(DEPTH):
        j = i // N_MIXERS
        hn = rms_norm(h, mix_norm[i])
        if i % N_MIXERS == 0:
            h = h + sgu_mixer(hn, sgu_w_in[j], sgu_v_gain[j], sgu_w_s[j], sgu_b_s[j], sgu_w_out[j])
        else:
            h = h + swa_mixer(hn, attn_w_qkv[j], attn_q_gain[j], attn_k_gain[j], attn_sinks[j],
                              attn_w_o[j], rel_bias)
        h = h + conv_glu_ffn(rms_norm(h, ffn_norm[i]), ffn_w_up[i], ffn_conv_w[i], ffn_conv_b[i], ffn_w_down[i])
    return h


_drawn_inputs = setup_inputs


def setup_inputs(seed=0):
    import zlib

    import numpy as np

    out = dict(_drawn_inputs(seed))
    spreads = {}
    factors = {'sgu_v_gain': 2.731,
     'attn_q_gain': 8.0,
     'attn_k_gain': 8.0,
     'attn_sinks': 64.0,
     'ffn_conv_b': 3.251}
    for name, (base, spread) in spreads.items():
        noise = np.random.default_rng([zlib.crc32(name.encode()), seed]).standard_normal(out[name].shape)
        drawn = base * np.exp(spread * noise) if base else spread * noise
        out[name] = __import__('jax').numpy.asarray(drawn.astype(out[name].dtype))
    for name, factor in factors.items():
        out[name] = (out[name] * factor).astype(out[name].dtype)
    return out
```

```python
import math
from contextlib import ExitStack

import numpy as np

import concourse.bass as bass
from concourse import mybir

F32 = mybir.dt.float32
F32R = mybir.dt.float32r
ALU = mybir.AluOpType
ACT = mybir.ActivationFunctionType
AX_X = mybir.AxisListType.X

P = 128
D_MODEL = 1024
SEQ = 512
KT = D_MODEL // P
TT = SEQ // P
GROUPS = 16
HEADS = 16
KV_HEADS = 4
HD = 64
D_FF = 2816
PAIRS = D_FF // P
BUCKETS = 32
MAX_DIST = 128
EPS = 1e-6
MASKED = -1e30

CHUNK = 1024
C_V = 0
C_U = C_V + 16
C_OUT = C_U + 16
C_UP0 = C_OUT + 2 * KT
C_DN0 = C_UP0 + 2 * PAIRS
C_KV = C_DN0 + 3 * KT
C_Q = C_KV + 4
C_WO = C_Q + KT
C_UP1 = C_WO + KT
C_DN1 = C_UP1 + 2 * PAIRS
CHUNKS = C_DN1 + 3 * KT
RING = 4
RAW = 2
AHEAD = 3

G_V, G_U, G_UP0, G_KV, G_Q, G_UP1 = 0, 16, 32, 76, 80, 88
A_S, A_OUT, A_DN0, A_WO, A_DN1 = 0, 16, 24, 32, 40
MISC = 7

PC_MIX, PC_FFN, PC_VG, PC_CONV = 0, 2 * KT, 4 * KT, 4 * KT + GROUPS
PC_ALL = PC_CONV + 2 * 2 * PAIRS * 4
PR_QG, PR_KG, PR_SINK, PR_ALL = 0, HD, 2 * HD, 2 * HD + HEADS

SLOT_Q, SLOT_K, SLOT_V, SLOT_P, SLOT_O = 0, 8, 10, 12, 14
UNITS = 2 * TT * 4


def rolled(eng, n, body):
    body(0, True, n == 1)
    if n > 3:
        with eng.Fori(1, n - 1) as i:
            body(i, False, False)
    else:
        for i in range(1, n - 1):
            body(i, False, False)
    if n > 1:
        body(n - 1, False, True)


def build(nc, x_t, stream, cols, rows, ws_t, b_s, rel, onehot, masked, out_t):
    ctx = ExitStack()
    with ctx:
        def sb(name, shape, dt=F32):
            return ctx.enter_context(nc.sbuf_tensor(name, shape, dt))

        def sem(name):
            return ctx.enter_context(nc.semaphore(name))

        ps = ctx.enter_context(nc.psum_tensor("ps", [P, 8, 512], F32))
        h = sb("h", [P, KT, SEQ])
        hn_h = sb("hn_h", [P, KT, SEQ], F32R)
        hn_l = sb("hn_l", [P, KT, SEQ], F32R)
        act_h = sb("act_h", [P, PAIRS, SEQ], F32R)
        act_l = sb("act_l", [P, PAIRS, SEQ], F32R)
        raw = sb("raw", [P, RAW, CHUNK])
        w_h = sb("w_h", [P, RING, CHUNK], F32R)
        w_l = sb("w_l", [P, RING, CHUNK], F32R)
        work = sb("work", [P, 5632])
        r_row = sb("r_row", [P, SEQ])
        ident = sb("ident", [P, P])
        ones = sb("ones", [P, P])
        halves = sb("halves", [P, 2])
        colp = sb("colp", [P, PC_ALL])
        rowp = sb("rowp", [P, PR_ALL])
        negsink = sb("negsink", [P, HEADS])
        qk_gain = sb("qk_gain", [P, HD])
        half_neg = sb("half_neg", [P, 64])
        mean = sb("mean", [P, 64])
        r_col = sb("r_col", [P, TT])
        r_v = sb("r_v", [P, TT])
        r2_col = sb("r2_col", [P, TT])
        r8_col = sb("r8_col", [P, TT])
        v_sq = sb("v_sq", [P, TT, 4])
        r_k = sb("r_k", [P, TT * KV_HEADS])
        r_q = sb("r_q", [P, 64])
        soft = sb("soft", [P, 6, 2 * UNITS])

        sq = work[:, 4608:5120]
        sq_sum = work[:, 5120:5632]
        diag = sq.rearrange("p (t q) -> p t q", t=TT)
        ff_a = work[:, 0:2 * 514].rearrange("p (r n) -> p r n", r=2)
        ff_c = work[:, 1028:1028 + 2048].rearrange("p (r n) -> p r n", r=4)
        ff_p = work[:, 3076:3076 + 1024].rearrange("p (r n) -> p r n", r=2)
        sg_a = work[:, 0:1024].rearrange("p (r n) -> p r n", r=2)
        sg_u = work[:, 1024:2048].rearrange("p (r n) -> p r n", r=2)
        sg_w = work[:, 2048:3072].rearrange("p (r n) -> p r n", r=2)
        sg_s = work[:, 3072:3584]
        ring_w = work[:, 3584:4096].rearrange("p (r n) -> p r n", r=4)
        ring_b = work[:, 4096:4608].rearrange("p (r n) -> p r n", r=4)
        at_bias = work[:, 0:4096].rearrange("p (g n) -> p g n", g=HEADS)
        at_s = work[:, 4096:5120].rearrange("p (r x n) -> p r x n", r=2, x=2)
        kv = work[:, 0:2048].rearrange("p (t n) -> p t n", t=TT)
        kv_sq = work[:, 2048:2560].rearrange("p (r n) -> p r n", r=2)
        q_sq = work[:, 2560:3584].rearrange("p (r n) -> p r n", r=2)
        k_n = work[:, 3584:4608].rearrange("p (t n) -> p t n", t=TT)
        rel_sb = work[0:BUCKETS, 0:HEADS]
        onehot_sb = work[0:BUCKETS, 512:896]
        masked_sb = work[0:HEADS, 1024:1408]
        line_sb = work[0:HEADS, 1536:1920]
        v_h = act_h[:, SLOT_V:SLOT_V + 2, :].rearrange("p s n -> p (s n)")
        v_l = act_l[:, SLOT_V:SLOT_V + 2, :].rearrange("p s n -> p (s n)")

        lines = nc.dram_tensor("rel_lines", (HEADS, P, 384), F32, kind="Internal").ap()

        params_landed = sem("params_landed")
        rel_landed = sem("rel_landed")
        x_landed = [sem(f"x_landed{d}") for d in range(KT)]
        raw_landed = [sem(f"raw_landed{s}") for s in range(RAW)]
        ws_landed = [sem(f"ws_landed{s}") for s in range(4)]
        b_landed = [sem(f"b_landed{s}") for s in range(4)]
        lines_stored = sem("lines_stored")
        bias_landed = sem("bias_landed")
        out_stored = sem("out_stored")
        hi_split = sem("hi_split")
        lo_split = sem("lo_split")
        chunk_used = sem("chunk_used")
        main_free = sem("main_free")
        out_free = sem("out_free")
        consts_zeroed = sem("consts_zeroed")
        consts_ready = sem("consts_ready")
        halves_ready = sem("halves_ready")
        gains_ready = sem("gains_ready")
        lines_summed = sem("lines_summed")
        lines_ready = sem("lines_ready")
        pads_zeroed = sem("pads_zeroed")
        hn_hi = sem("hn_hi")
        hn_lo = sem("hn_lo")
        squared = sem("squared")
        sq_added = sem("sq_added")
        col_summed = sem("col_summed")
        mean_ready = sem("mean_ready")
        r_ready = sem("r_ready")
        diag_ready = sem("diag_ready")
        row_spread = sem("row_spread")
        row_ready = sem("row_ready")
        v_full = sem("v_full")
        v_gelu = sem("v_gelu")
        v_squared = sem("v_squared")
        v_hi = sem("v_hi")
        v_lo = sem("v_lo")
        v_sum = sem("v_sum")
        vmean_ready = sem("vmean_ready")
        rv_ready = sem("rv_ready")
        ws_masked = sem("ws_masked")
        wr_scaled = sem("wr_scaled")
        wr_hi = sem("wr_hi")
        wr_lo = sem("wr_lo")
        u_gelu = sem("u_gelu")
        mix_full = sem("mix_full")
        gated = sem("gated")
        gated_hi = sem("gated_hi")
        gated_lo = sem("gated_lo")
        conv_0 = sem("conv_0")
        conv_1 = sem("conv_1")
        conv_2 = sem("conv_2")
        silu_done = sem("silu_done")
        prod = sem("prod")
        prod_hi = sem("prod_hi")
        prod_lo = sem("prod_lo")
        kv_full = sem("kv_full")
        vv_hi = sem("vv_hi")
        vv_lo = sem("vv_lo")
        k_squared = sem("k_squared")
        k_ss = sem("k_ss")
        k_mean = sem("k_mean")
        rk_ready = sem("rk_ready")
        k_scaled = sem("k_scaled")
        k_normed = sem("k_normed")
        k_turned = sem("k_turned")
        kt_hi = sem("kt_hi")
        kt_lo = sem("kt_lo")
        q_hi = sem("q_hi")
        q_squared = sem("q_squared")
        q_summed = sem("q_summed")
        rx_ready = sem("rx_ready")
        q_scaled = sem("q_scaled")
        q_mean = sem("q_mean")
        q_pow = sem("q_pow")
        rq_ready = sem("rq_ready")
        s_full = sem("s_full")
        s_biased = sem("s_biased")
        s_max = sem("s_max")
        m_ready = sem("m_ready")
        sink_off = sem("sink_off")
        p_exp = sem("p_exp")
        sink_exp = sem("sink_exp")
        den = sem("den")
        rden = sem("rden")
        p_scaled = sem("p_scaled")
        p_turned = sem("p_turned")
        p_hi = sem("p_hi")
        p_lo = sem("p_lo")
        o_full = sem("o_full")
        o_hi = sem("o_hi")
        o_lo = sem("o_lo")

        block = ctx.enter_context(nc.Block())

        def operand_blocks(kb):
            return slice(kb * P, (kb + 1) * P)

        def settle(eng):
            eng.wait_ge(params_landed, 16 * 2)

        @block.sync
        def _(sp):
            def load(c, slot, again):
                if again:
                    sp.wait_ge(lo_split, c - RAW + 1)
                sp.dma_start(raw[:, slot, :], stream[c]).then_inc(raw_landed[slot], 16)

            for d in range(2):
                sp.dma_start(h[:, d, :], x_t[d]).then_inc(x_landed[d], 16)
            sp.dma_start(colp[:], cols).then_inc(params_landed, 16)
            load(0, 0, False)
            load(1, 1, False)
            for d in range(2, KT):
                sp.dma_start(h[:, d, :], x_t[d]).then_inc(x_landed[d], 16)
            sp.dma_start(rowp[:], rows.partition_broadcast(P)).then_inc(params_landed, 16)
            with sp.Fori(1, CHUNKS // RAW) as i:
                for k in range(RAW):
                    load(RAW * i + k, k, True)
            for d in range(KT):
                sp.wait_ge(out_free, A_DN1 + d + 1)
                sp.dma_start(out_t[d], h[:, d, :]).then_inc(out_stored, 16)
            sp.wait_ge(out_stored, 16 * KT)

        @block.gpsimd
        def _(pool):
            pool.memset(ident[:], 0.0).then_inc(consts_zeroed, 1)
            pool.wait_ge(consts_zeroed, 1)
            pool.affine_select(out=ident[:], in_=ident[:], compare_op=ALU.not_equal, fill=1.0, base=0,
                               pattern=[[-1, P]], channel_multiplier=1).then_inc(consts_ready, 1)
            pool.memset(ones[:], 1.0).then_inc(consts_ready, 1)
            pool.memset(half_neg[:], -0.5).then_inc(consts_ready, 1)
            pool.wait_ge(consts_ready, 3)

            pool.dma_start(rel_sb, rel).then_inc(rel_landed, 16)
            pool.dma_start(onehot_sb, onehot).then_inc(rel_landed, 16)
            pool.dma_start(masked_sb, masked).then_inc(rel_landed, 16)
            pool.wait_ge(lines_ready, 1)
            pool.dma_start(lines, line_sb.unsqueeze(1).broadcast_to([HEADS, P, 384]))\
                .then_inc(lines_stored, 16)

            def root(n_sem, n, dst, width, done):
                pool.wait_ge(n_sem, n)
                pool.tensor_tensor(dst, mean[:, 0:width], half_neg[:, 0:width], ALU.pow)\
                    .then_inc(done, 1)

            root(mean_ready, 1, r_col[:], TT, r_ready)

            def fetch(g, s, again):
                if again:
                    pool.wait_ge(wr_scaled, g - 3)
                    pool.wait_ge(out_free, A_S + g - 3)
                pool.dma_start(ring_w[:, s, :], ws_t[g]).then_inc(ws_landed[s], 16)
                pool.dma_start(ring_b[:, s, :], b_s[g].partition_broadcast(P)).then_inc(b_landed[s], 16)

            def mask(g, s, turn):
                pool.wait_ge(ws_landed[s], 16 * (turn + 1))
                settle(pool)
                pool.affine_select(out=ring_w[:, s, :], in_=ring_w[:, s, :], compare_op=ALU.is_ge, fill=0.0,
                                   base=0, pattern=[[1, P]], channel_multiplier=-1).then_inc(ws_masked, 1)

            pool.wait_ge(lines_stored, 16)
            for g in range(4):
                fetch(g, g, False)
            for g in range(4):
                mask(g, g, 0)
            root(vmean_ready, 1, r_v[:], TT, rv_ready)
            for i in range(1, GROUPS // 4):
                for s in range(4):
                    fetch(4 * i + s, s, True)
                    mask(4 * i + s, s, i)
            root(mean_ready, 2, r_col[:], TT, r_ready)
            root(mean_ready, 3, r_col[:], TT, r_ready)
            root(k_mean, 1, r_k[:], TT * KV_HEADS, rk_ready)
            pool.wait_ge(k_turned, 8)
            pool.wait_ge(q_summed, KT)
            pool.wait_ge(vv_lo, TT)
            pool.dma_start(at_bias, bass.AP(lines.tensor, P - 1, [[383, P], [P * 384, HEADS], [1, 256]]))\
                .then_inc(bias_landed, 16)
            root(q_mean, 1, r_q[:], 64, q_pow)
            root(mean_ready, 4, r_col[:], TT, r_ready)

        @block.scalar
        def _(act):
            def tick(c, slot):
                if isinstance(c, int) and c + AHEAD >= CHUNKS:
                    return
                split(c + AHEAD, (slot + AHEAD) % RING, True)

            def split(c, slot, again):
                act.wait_ge(raw_landed[slot % RAW], 16 * (c // RAW + 1) if isinstance(c, int)
                            else (c - slot % RAW) * (16 // RAW) + 16)
                if again and not (isinstance(c, int) and c < RING):
                    act.wait_ge(chunk_used, c - RING + 1)
                act.activation(w_h[:, slot, :], raw[:, slot % RAW, :], ACT.Copy).then_inc(hi_split, 1)

            def spread_hi(n, d, gain, ready, count, first):
                if not first:
                    act.wait_ge(sq_added, KT * n + d)
                act.wait_ge(ready, count)
                settle(act)
                act.activation(hn_h[:, d, :], h[:, d, :], ACT.Copy, scale=gain).then_inc(hn_hi, 1)
                act.activation(sq, h[:, d, :], ACT.Square).then_inc(squared, 1)

            def project(n, base, a_base, chunks, gain_col):
                per = {3: 4, 2: 2, 1: 4}[chunks]

                def body(i, first, last):
                    for dd in range(per):
                        d = i * per + dd
                        for k in range(chunks):
                            tick(base + (i * per + dd) * chunks + k, (dd * chunks + k) % RING)
                        if n < 4:
                            spread_hi(n, d, colp[:, gain_col + d:gain_col + d + 1] if isinstance(d, int)
                                      else colp[:, bass.ds(gain_col + d, 1)], out_free, a_base + d + 1,
                                      first and dd == 0)

                rolled(act, KT // per, body)

            def ffn(layer, base, g_base):
                def body(i, first, last):
                    for k in range(4):
                        tile = 4 * i + k
                        g = g_base + tile
                        n = 44 * layer + tile
                        pair = PAIRS * layer + 2 * i + k // 2
                        if k % 2 == 0 and not (first and k == 0):
                            pp = 2 * i + k // 2 - 1
                            act.wait_ge(prod, pair)
                            settle(act)
                            act.activation(act_h[:, pp, :], ff_p[:, (k // 2 + 1) % 2, :], ACT.Copy)\
                                .then_inc(prod_hi, 1)
                        if not (first and k < 2):
                            tick(base + tile, k)
                        if k % 2 == 1:
                            act.wait_ge(conv_2, n)
                            act.activation(ff_c[:, k - 1, :], ff_c[:, k - 1, :], ACT.Silu)\
                                .then_inc(silu_done, 1)
                        act.wait_ge(main_free, g + 1)
                        if not (first and layer == 0):
                            act.wait_ge(prod, pair - 1)
                        settle(act)
                        pc = PC_CONV + 4 * (44 * layer + tile)
                        act.activation(ff_c[:, k, :], ff_a[:, k % 2, 2:514], ACT.Identity,
                                       bias=colp[:, bass.ds(pc + 3, 1)], scale=colp[:, bass.ds(pc + 2, 1)])\
                            .then_inc(conv_0, 1)

                tick(base, 0)
                tick(base + 1, 1)
                rolled(act, PAIRS // 2, body)
                act.wait_ge(prod, PAIRS * (layer + 1))
                act.activation(act_h[:, PAIRS - 1, :], ff_p[:, 1, :], ACT.Copy).then_inc(prod_hi, 1)

            act.wait_ge(params_landed, 16 * 2)
            for d in range(KT):
                act.wait_ge(x_landed[d], 16)
                spread_hi(0, d, colp[:, PC_MIX + d:PC_MIX + d + 1], x_landed[d], 16, d == 0)
                if d % 3 == 0:
                    split(d // 3, d // 3, False)

            def v_block(j, first, last):
                for q in range(4):
                    tick(C_V + 4 * j + q, q)
                for t in range(TT):
                    u = 4 * j + t
                    act.wait_ge(main_free, G_V + u + 1)
                    if not (first and t < 2):
                        act.wait_ge(v_lo, u - 1)
                    act.activation(sg_u[:, t % 2, :], sg_a[:, t % 2, :], ACT.Gelu).then_inc(v_gelu, 1)
                    act.wait_ge(v_gelu, u + 1)
                    settle(act)
                    act.activation(sg_w[:, 0, :], sg_u[:, t % 2, :], ACT.Square,
                                   accum_out=v_sq[:, t, bass.ds(j, 1)]).then_inc(v_squared, 1)
                    act.activation(act_h[:, bass.ds(4 * j, 4), t * P:(t + 1) * P],
                                   sg_u[:, t % 2, :].rearrange("p (g d) -> p g d", g=4), ACT.Copy)\
                        .then_inc(v_hi, 1)
                    act.wait_ge(v_squared, u + 1)

            rolled(act, 4, v_block)

            def wr_part(g, par):
                act.wait_ge(wr_scaled, g + 1)
                if not (isinstance(g, int) and g < 2):
                    act.wait_ge(mix_full, g - 1)
                act.activation(act_h[:, 16 + par, :], sg_w[:, par, :], ACT.Copy).then_inc(wr_hi, 1)

            def gate_hi(g):
                act.wait_ge(gated, g + 1)
                settle(act)
                act.activation(act_h[:, g, :], sg_s, ACT.Copy).then_inc(gated_hi, 1)

            wr_part(0, 0)

            def u_block(i, first, last):
                for k in range(4):
                    g = 4 * i + k
                    tick(C_U + g, k)
                    act.wait_ge(main_free, G_U + g + 1)
                    if not (first and k < 2):
                        act.wait_ge(gated, g - 1)
                    act.activation(sg_u[:, k % 2, :], sg_a[:, k % 2, :], ACT.Gelu).then_inc(u_gelu, 1)
                    if not (last and k == 3):
                        wr_part(g + 1, (k + 1) % 2)
                    if not (first and k == 0):
                        gate_hi(g - 1)

            rolled(act, GROUPS // 4, u_block)
            gate_hi(GROUPS - 1)
            project(1, C_OUT, A_OUT, 2, PC_FFN)
            ffn(0, C_UP0, G_UP0)
            project(2, C_DN0, A_DN0, 3, PC_MIX + KT)

            for q in range(4):
                tick(C_KV + q, q)
            for t in range(TT):
                act.wait_ge(main_free, G_KV + t + 1)
                act.activation(v_h[:, t * 256:(t + 1) * 256], kv[:, t, 256:512], ACT.Copy).then_inc(vv_hi, 1)
                if t >= 2:
                    act.wait_ge(k_ss, t - 1)
                act.activation(kv_sq[:, t % 2, :], kv[:, t, 0:256], ACT.Square).then_inc(k_squared, 1)

            for i in range(KT):
                tick(C_Q + i, i % 4)
                act.wait_ge(chunk_used, C_Q + i + 1)
                act.activation(act_h[:, SLOT_Q + i, :], ps[:, i % 4, :], ACT.Copy).then_inc(q_hi, 1)
                if i >= 2:
                    act.wait_ge(q_summed, i - 1)
                act.activation(q_sq[:, i % 2, :], ps[:, i % 4, :], ACT.Square).then_inc(q_squared, 1)
                if i == 2:
                    for c in range(2):
                        act.wait_ge(k_turned, 4 * c + 4)
                        act.activation(act_h[:, SLOT_K + c, :], ps[:, 5 + c, :], ACT.Copy).then_inc(kt_hi, 1)

            def attend(u):
                if u < UNITS:
                    first_key = P if (u // 4) % TT == 0 else 0
                    act.wait_ge(sink_off, u + 1)
                    for x in range(2):
                        s = at_s[:, u % 2, x, first_key:]
                        act.activation(s, s, ACT.Exp, bias=soft[:, 0, 2 * u + x:2 * u + x + 1],
                                       accum_out=soft[:, 2, 2 * u + x:2 * u + x + 1]).then_inc(p_exp, 1)
                    act.activation(soft[:, 3, 2 * u:2 * u + 2], soft[:, 1, 2 * u:2 * u + 2], ACT.Exp)\
                        .then_inc(sink_exp, 1)
                if 2 <= u < UNITS + 2:
                    w = u - 2
                    first_half = 256 if (w // 4) % TT == 0 else 0
                    act.wait_ge(p_turned, w + 1)
                    if w >= 2:
                        act.wait_ge(o_full, w - 1)
                    act.activation(act_h[:, SLOT_P + w % 2, first_half:], ps[:, 4 + w % 2, first_half:],
                                   ACT.Copy).then_inc(p_hi, 1)
                if u >= 3:
                    w = u - 3
                    c, n, i = w // 16, (w // 4) % TT, w % 4
                    act.wait_ge(o_full, w + 1)
                    for x in range(2):
                        part = slice(x * HD, (x + 1) * HD)
                        act.activation(act_h[part, SLOT_O + 4 * c + i, n * P:(n + 1) * P],
                                       ps[part, 6 + w % 2, x * P:(x + 1) * P],
                                       ACT.Copy).then_inc(o_hi, 1)

            for u in range(UNITS + 3):
                attend(u)
            project(3, C_WO, A_WO, 1, PC_FFN + KT)
            ffn(1, C_UP1, G_UP1)
            project(4, C_DN1, A_DN1, 3, 0)

        @block.vector
        def _(dve):
            def tick(c, slot):
                if isinstance(c, int) and c + AHEAD >= CHUNKS:
                    return
                split(c + AHEAD, (slot + AHEAD) % RING)

            def split(c, slot):
                dve.wait_ge(hi_split, c + 1)
                dve.tensor_tensor(w_l[:, slot, :], raw[:, slot % RAW, :], w_h[:, slot, :].bitcast(F32),
                                  ALU.subtract).then_inc(lo_split, 1)

            def spread_lo(n, d, gain, first):
                dve.wait_ge(hn_hi, KT * n + d + 1)
                dve.scalar_tensor_tensor(out=hn_l[:, d, :], in0=h[:, d, :], scalar=gain,
                                         in1=hn_h[:, d, :].bitcast(F32), op0=ALU.mult, op1=ALU.subtract)\
                    .then_inc(hn_lo, 1)
                dve.wait_ge(squared, KT * n + d + 1)
                if first:
                    dve.tensor_copy(sq_sum, sq).then_inc(sq_added, 1)
                else:
                    dve.wait_ge(sq_added, KT * n + d)
                    dve.tensor_tensor(sq_sum, sq_sum, sq, ALU.add).then_inc(sq_added, 1)

            def finish_norm(n, c):
                tick(c, 0)
                dve.wait_ge(col_summed, n + 1)
                dve.tensor_scalar(mean[:, 0:TT], ps[:, MISC, 0:TT], 1.0 / D_MODEL, EPS, ALU.mult, ALU.add)\
                    .then_inc(mean_ready, 1)
                dve.wait_ge(r_ready, n + 1)
                dve.tensor_tensor(diag, ident[:].unsqueeze(1).broadcast_to([P, TT, P]),
                                  r_col[:].unsqueeze(2).broadcast_to([P, TT, P]), ALU.mult)\
                    .then_inc(diag_ready, 1)
                tick(c + 1, 1)
                dve.wait_ge(row_spread, n + 1)
                dve.tensor_copy(r_row[:], ps[:, MISC, :]).then_inc(row_ready, 1)
                dve.wait_ge(row_ready, n + 1)

            def project(n, base, a_base, chunks, gain_col):
                per = {3: 4, 2: 2, 1: 4}[chunks]

                def body(i, first, last):
                    for dd in range(per):
                        d = i * per + dd
                        for k in range(chunks):
                            tick(base + (i * per + dd) * chunks + k, (dd * chunks + k) % RING)
                        dve.wait_ge(chunk_used, base + (d + 1) * chunks)
                        dve.tensor_tensor(h[:, d, :], ps[:, 4 + dd % 2, :], h[:, d, :], ALU.add)\
                            .then_inc(out_free, 1)
                        if n < 4:
                            dve.wait_ge(out_free, a_base + d + 1)
                            spread_lo(n, d, colp[:, bass.ds(gain_col + d, 1)], first and dd == 0)

                rolled(dve, KT // per, body)

            def ffn(layer, base, g_base):
                def product_lo(pair, pp, par):
                    dve.wait_ge(prod_hi, pair + 1)
                    dve.tensor_tensor(act_l[:, pp, :], ff_p[:, par, :], act_h[:, pp, :].bitcast(F32),
                                      ALU.subtract).then_inc(prod_lo, 1)

                def body(i, first, last):
                    for k in range(4):
                        tile = 4 * i + k
                        n = 44 * layer + tile
                        pair = PAIRS * layer + 2 * i + k // 2
                        pc = PC_CONV + 4 * (44 * layer + tile)
                        dve.wait_ge(chunk_used, base + tile + 1)
                        if not (first and layer == 0 and k < 2):
                            dve.wait_ge(conv_0, n - 1)
                        dve.tensor_tensor(ff_a[:, k % 2, 2:514], ps[:, k, :], r_row[:], ALU.mult)\
                            .then_inc(main_free, 1)
                        if k % 2 == 0 and not (first and k == 0):
                            product_lo(pair - 1, 2 * i + k // 2 - 1, (k // 2 + 1) % 2)
                        if not (first and k < 2):
                            tick(base + tile, k)
                        dve.wait_ge(conv_0, n + 1)
                        dve.scalar_tensor_tensor(out=ff_c[:, k, :], in0=ff_a[:, k % 2, 1:513],
                                                 scalar=colp[:, bass.ds(pc + 1, 1)], in1=ff_c[:, k, :],
                                                 op0=ALU.mult, op1=ALU.add).then_inc(conv_1, 1)
                        dve.wait_ge(conv_1, n + 1)
                        dve.scalar_tensor_tensor(out=ff_c[:, k, :], in0=ff_a[:, k % 2, 0:512],
                                                 scalar=colp[:, bass.ds(pc, 1)], in1=ff_c[:, k, :],
                                                 op0=ALU.mult, op1=ALU.add).then_inc(conv_2, 1)
                        if k % 2 == 1:
                            dve.wait_ge(silu_done, pair + 1)
                            dve.wait_ge(conv_2, n + 1)
                            dve.tensor_tensor(ff_p[:, k // 2, :], ff_c[:, k - 1, :], ff_c[:, k, :],
                                              ALU.mult).then_inc(prod, 1)

                finish_norm(1 if layer == 0 else 3, base)
                dve.memset(ff_a[:, :, 0:2], 0.0).then_inc(pads_zeroed, 1)
                dve.wait_ge(pads_zeroed, layer + 1)
                rolled(dve, PAIRS // 2, body)
                product_lo(PAIRS * (layer + 1) - 1, PAIRS - 1, 1)

            dve.memset(halves[:], 0.0).then_inc(halves_ready, 1)
            dve.wait_ge(halves_ready, 1)
            dve.memset(halves[0:HD, 0:1], 1.0).then_inc(halves_ready, 1)
            dve.memset(halves[HD:P, 1:2], 1.0).then_inc(halves_ready, 1)
            dve.wait_ge(params_landed, 16 * 2)
            for d in range(KT):
                dve.wait_ge(x_landed[d], 16)
                spread_lo(0, d, colp[:, PC_MIX + d:PC_MIX + d + 1], d == 0)
                if d % 3 == 0:
                    split(d // 3, d // 3)
            dve.tensor_scalar(negsink[:], rowp[:, PR_SINK:PR_ALL], -1.0, None, ALU.mult)\
                .then_inc(gains_ready, 1)
            dve.tensor_tensor(qk_gain[:], rowp[:, PR_QG:PR_QG + HD], rowp[:, PR_KG:PR_KG + HD], ALU.mult)\
                .then_inc(gains_ready, 1)
            dve.wait_ge(lines_summed, 1)
            dve.tensor_tensor(line_sb, ps[0:HEADS, 6, 0:384], masked_sb, ALU.add).then_inc(lines_ready, 1)
            finish_norm(0, C_V)
            dve.wait_ge(lines_stored, 16)

            def v_lo_part(j, t):
                u = 4 * j + t
                dve.wait_ge(v_hi, u + 1)
                dve.tensor_tensor(act_l[:, bass.ds(4 * j, 4), t * P:(t + 1) * P],
                                  sg_u[:, t % 2, :].rearrange("p (g d) -> p g d", g=4),
                                  act_h[:, bass.ds(4 * j, 4), t * P:(t + 1) * P].bitcast(F32),
                                  ALU.subtract).then_inc(v_lo, 1)

            def v_block(j, first, last):
                for q in range(4):
                    if not (first and q < 2):
                        tick(C_V + 4 * j + q, q)
                for t in range(TT):
                    u = 4 * j + t
                    if t < TT - 1:
                        dve.wait_ge(v_full, 3 * j + t + 1)
                    else:
                        dve.wait_ge(chunk_used, C_V + 4 * j + 4)
                    if not (first and t < 2):
                        dve.wait_ge(v_gelu, u - 1)
                    dve.tensor_scalar(sg_a[:, t % 2, :], ps[:, t, :], r_col[:, t:t + 1], None, ALU.mult)\
                        .then_inc(main_free, 1)
                    if t >= 1:
                        v_lo_part(j, t - 1)
                v_lo_part(j, TT - 1)

            rolled(dve, 4, v_block)

            dve.wait_ge(v_squared, 4 * TT)
            dve.tensor_reduce(mean[:, 8:8 + TT], v_sq[:], AX_X, ALU.add).then_inc(v_sum, 1)
            dve.wait_ge(v_sum, 1)
            dve.tensor_scalar(mean[:, 0:TT], mean[:, 8:8 + TT], 1.0 / (GROUPS * P), EPS, ALU.mult, ALU.add)\
                .then_inc(vmean_ready, 1)
            dve.wait_ge(rv_ready, 1)

            def wr_scale(g, par, slot):
                dve.wait_ge(ws_masked, g + 1)
                if not (isinstance(g, int) and g < 2):
                    dve.wait_ge(wr_lo, g - 1)
                dve.tensor_tensor(sg_w[:, par, :].rearrange("p (c t) -> p c t", c=TT),
                                  ring_w[:, slot, :].unsqueeze(1).broadcast_to([P, TT, P]),
                                  r_v[:].unsqueeze(2).broadcast_to([P, TT, P]), ALU.mult)\
                    .then_inc(wr_scaled, 1)

            def wr_part(g, par):
                dve.wait_ge(wr_hi, g + 1)
                dve.tensor_tensor(act_l[:, 16 + par, :], sg_w[:, par, :], act_h[:, 16 + par, :].bitcast(F32),
                                  ALU.subtract).then_inc(wr_lo, 1)

            def mix(g, par, slot, turn):
                dve.wait_ge(mix_full, g + 1)
                dve.wait_ge(b_landed[slot], 16 * (turn + 1))
                if not (isinstance(g, int) and g == 0):
                    dve.wait_ge(gated_lo, g)
                dve.scalar_tensor_tensor(out=sg_s.rearrange("p (c t) -> p c t", c=TT),
                                         in0=ps[:, 4 + par, :].rearrange("p (c t) -> p c t", c=TT),
                                         scalar=colp[:, bass.ds(PC_VG + g, 1)],
                                         in1=ring_b[:, slot, :].unsqueeze(1).broadcast_to([P, TT, P]),
                                         op0=ALU.mult, op1=ALU.add).then_inc(out_free, 1)
                dve.wait_ge(out_free, A_S + g + 1)
                dve.wait_ge(u_gelu, g + 1)
                dve.tensor_tensor(sg_s, sg_s, sg_u[:, par, :], ALU.mult).then_inc(gated, 1)

            def gate_lo(g):
                dve.wait_ge(gated_hi, g + 1)
                dve.tensor_tensor(act_l[:, g, :], sg_s, act_h[:, g, :].bitcast(F32), ALU.subtract)\
                    .then_inc(gated_lo, 1)

            wr_scale(0, 0, 0)
            wr_part(0, 0)

            def u_block(i, first, last):
                for k in range(4):
                    g = 4 * i + k
                    tick(C_U + g, k)
                    dve.wait_ge(chunk_used, C_U + g + 1)
                    if not (first and k < 2):
                        dve.wait_ge(u_gelu, g - 1)
                    dve.tensor_tensor(sg_a[:, k % 2, :], ps[:, k, :], r_row[:], ALU.mult).then_inc(main_free, 1)
                    if not (last and k == 3):
                        wr_scale(g + 1, (k + 1) % 2, (k + 1) % 4)
                    if not (first and k == 0):
                        mix(g - 1, (k + 1) % 2, (k + 3) % 4, i - 1 if k == 0 else i)
                    if not (last and k == 3):
                        wr_part(g + 1, (k + 1) % 2)
                    if not (first and k == 0):
                        gate_lo(g - 1)

            rolled(dve, GROUPS // 4, u_block)
            mix(GROUPS - 1, 1, 3, 3)
            gate_lo(GROUPS - 1)
            project(1, C_OUT, A_OUT, 2, PC_FFN)
            ffn(0, C_UP0, G_UP0)
            project(2, C_DN0, A_DN0, 3, PC_MIX + KT)

            finish_norm(2, C_KV)
            dve.tensor_tensor(r2_col[:], r_col[:], r_col[:], ALU.mult).then_inc(rx_ready, 1)
            dve.tensor_scalar(r8_col[:], r_col[:], HD ** -0.5, None, ALU.mult).then_inc(rx_ready, 1)
            for q in range(2, 4):
                tick(C_KV + q, q)
            for t in range(TT):
                if t < TT - 1:
                    dve.wait_ge(kv_full, t + 1)
                else:
                    dve.wait_ge(chunk_used, C_KV + 4)
                dve.tensor_scalar(kv[:, t, :], ps[:, t, :], r_col[:, t:t + 1], None, ALU.mult)\
                    .then_inc(main_free, 1)
                dve.wait_ge(vv_hi, t + 1)
                dve.tensor_tensor(v_l[:, t * 256:(t + 1) * 256], kv[:, t, 256:512],
                                  v_h[:, t * 256:(t + 1) * 256].bitcast(F32), ALU.subtract)\
                    .then_inc(vv_lo, 1)
                dve.wait_ge(k_squared, t + 1)
                dve.tensor_reduce(mean[:, 32 + 4 * t:36 + 4 * t],
                                  kv_sq[:, t % 2, :].rearrange("p (g d) -> p g d", g=KV_HEADS), AX_X, ALU.add)\
                    .then_inc(k_ss, 1)
            dve.wait_ge(k_ss, TT)
            dve.tensor_scalar(mean[:, 0:16], mean[:, 32:48], 1.0 / HD, EPS, ALU.mult, ALU.add)\
                .then_inc(k_mean, 1)
            tick(C_Q, 0)
            dve.wait_ge(rk_ready, 1)
            dve.wait_ge(gains_ready, 2)
            for t in range(TT):
                k_view = kv[:, t, 0:256].rearrange("p (g d) -> p g d", g=KV_HEADS)
                n_view = k_n[:, t, :].rearrange("p (g d) -> p g d", g=KV_HEADS)
                dve.tensor_tensor(k_view, k_view, r_k[:, 4 * t:4 * t + 4].unsqueeze(2)
                                  .broadcast_to([P, KV_HEADS, HD]), ALU.mult).then_inc(k_scaled, 1)
                dve.wait_ge(k_scaled, t + 1)
                dve.tensor_tensor(n_view, k_view, qk_gain[:].unsqueeze(1).broadcast_to([P, KV_HEADS, HD]),
                                  ALU.mult).then_inc(k_normed, 1)
            for i in range(KT):
                if i > 0:
                    tick(C_Q + i, i % 4)
                dve.wait_ge(q_squared, i + 1)
                dve.tensor_tensor(act_l[:, SLOT_Q + i, :], ps[:, i % 4, :], act_h[:, SLOT_Q + i, :].bitcast(F32),
                                  ALU.subtract).then_inc(main_free, 1)
                if i == 2:
                    for c in range(2):
                        dve.wait_ge(kt_hi, c + 1)
                        dve.tensor_tensor(act_l[:, SLOT_K + c, :], ps[:, 5 + c, :],
                                          act_h[:, SLOT_K + c, :].bitcast(F32), ALU.subtract)\
                            .then_inc(kt_lo, 1)
            dve.wait_ge(q_summed, KT)
            dve.wait_ge(rx_ready, 2)
            by_tile = [P, KT, TT, 2]
            r2 = r2_col[:].unsqueeze(1).unsqueeze(3).broadcast_to(by_tile)
            r8 = r8_col[:].unsqueeze(1).unsqueeze(3).broadcast_to(by_tile)
            tiles = lambda x: x.rearrange("p (i t x) -> p i t x", i=KT, t=TT)
            dve.tensor_tensor(tiles(r_q[:]), tiles(ps[:, MISC, 0:64]), r2, ALU.mult).then_inc(q_scaled, 1)
            dve.wait_ge(q_scaled, 1)
            dve.tensor_scalar(mean[:], r_q[:], 1.0 / HD, EPS, ALU.mult, ALU.add).then_inc(q_mean, 1)
            dve.wait_ge(q_pow, 1)
            dve.tensor_tensor(tiles(r_q[:]), tiles(r_q[:]), r8, ALU.mult).then_inc(rq_ready, 1)
            dve.wait_ge(rq_ready, 1)
            dve.wait_ge(bias_landed, 16)

            def attend(u):
                if u < UNITS:
                    c, n, i = u // 16, (u // 4) % TT, u % 4
                    first_key = P if n == 0 else 0
                    dve.wait_ge(s_full, u + 1)
                    if u >= 2:
                        dve.wait_ge(p_turned, u - 1)
                    col = (4 * c + i) * 8 + 2 * n
                    for x in range(2):
                        dve.scalar_tensor_tensor(out=at_s[:, u % 2, x, first_key:],
                                                 in0=ps[:, x + 2 * (u % 2), first_key:256],
                                                 scalar=r_q[:, col + x:col + x + 1],
                                                 in1=at_bias[:, 8 * c + 2 * i + x, first_key:],
                                                 op0=ALU.mult, op1=ALU.add).then_inc(s_biased, 1)
                    dve.wait_ge(s_biased, 2 * u + 2)
                    two = slice(2 * u, 2 * u + 2)
                    sink = slice(8 * c + 2 * i, 8 * c + 2 * i + 2)
                    dve.tensor_reduce(soft[:, 4, two], at_s[:, u % 2, :, first_key:], AX_X, ALU.max)\
                        .then_inc(s_max, 1)
                    dve.wait_ge(s_max, u + 1)
                    dve.scalar_tensor_tensor(out=soft[:, 0, two], in0=soft[:, 4, two], scalar=-1.0,
                                             in1=negsink[:, sink], op0=ALU.mult, op1=ALU.min)\
                        .then_inc(m_ready, 1)
                    dve.wait_ge(m_ready, u + 1)
                    dve.tensor_tensor(soft[:, 1, two], soft[:, 0, two],
                                      rowp[:, PR_SINK + 8 * c + 2 * i:PR_SINK + 8 * c + 2 * i + 2], ALU.add)\
                        .then_inc(sink_off, 1)
                if 1 <= u < UNITS + 1:
                    w = u - 1
                    first_key = P if (w // 4) % TT == 0 else 0
                    two = slice(2 * w, 2 * w + 2)
                    dve.wait_ge(sink_exp, w + 1)
                    dve.wait_ge(p_exp, 2 * w + 2)
                    dve.tensor_tensor(soft[:, 4, two], soft[:, 2, two], soft[:, 3, two], ALU.add).then_inc(den, 1)
                    dve.wait_ge(den, w + 1)
                    dve.reciprocal(soft[:, 5, two], soft[:, 4, two]).then_inc(rden, 1)
                    dve.wait_ge(rden, w + 1)
                    for x in range(2):
                        s = at_s[:, w % 2, x, first_key:]
                        dve.tensor_scalar(s, s, soft[:, 5, 2 * w + x:2 * w + x + 1], None, ALU.mult)\
                            .then_inc(p_scaled, 1)
                if 2 <= u < UNITS + 2:
                    w = u - 2
                    first_half = 256 if (w // 4) % TT == 0 else 0
                    dve.wait_ge(p_hi, w + 1)
                    dve.tensor_tensor(act_l[:, SLOT_P + w % 2, first_half:], ps[:, 4 + w % 2, first_half:],
                                      act_h[:, SLOT_P + w % 2, first_half:].bitcast(F32), ALU.subtract)\
                        .then_inc(p_lo, 1)
                if u >= 3:
                    w = u - 3
                    c, n, i = w // 16, (w // 4) % TT, w % 4
                    dve.wait_ge(o_hi, 2 * w + 2)
                    for x in range(2):
                        part = slice(x * HD, (x + 1) * HD)
                        dst = (part, SLOT_O + 4 * c + i, slice(n * P, (n + 1) * P))
                        dve.tensor_tensor(act_l[dst], ps[part, 6 + w % 2, x * P:(x + 1) * P],
                                          act_h[dst].bitcast(F32), ALU.subtract).then_inc(o_lo, 1)

            for u in range(UNITS + 3):
                attend(u)
            project(3, C_WO, A_WO, 1, PC_FFN + KT)
            ffn(1, C_UP1, G_UP1)
            project(4, C_DN1, A_DN1, 3, 0)

        @block.tensor
        def _(pe):
            def mm3(dst, stat_h, stat_l, mov_h, mov_l, start, stop):
                pe.matmul(dst, stat_h, mov_h, start=start, stop=False)
                pe.matmul(dst, stat_h, mov_l, start=False, stop=False)
                return pe.matmul(dst, stat_l, mov_h, start=False, stop=stop)

            def norm_sums(n):
                pe.wait_ge(sq_added, KT * (n + 1))
                for t in range(TT):
                    m = pe.matmul(ps[:, MISC, t:t + 1], sq_sum[:, t * P:(t + 1) * P], ones[:, 0:1],
                                  start=True, stop=True)
                m.then_inc(col_summed, 1)

            def norm_row(n):
                pe.wait_ge(diag_ready, n + 1)
                pe.matmul(ps[:, MISC, :], ones[:], sq, start=True, stop=True).then_inc(row_spread, 1)

            def tile_chunk(c, slot, bank, n, wait_tiles):
                pe.wait_ge(lo_split, c + 1)
                for k in range(KT):
                    if wait_tiles:
                        pe.wait_ge(hn_lo, KT * n + k + 1)
                    b = operand_blocks(k)
                    m = mm3(ps[:, bank, :], w_h[:, slot, b], w_l[:, slot, b], hn_h[:, k, :], hn_l[:, k, :],
                            k == 0, k == KT - 1)
                m.then_inc(chunk_used, 1)

            def token_chunk(c, q, full, wait_bank, wait_tiles, n):
                pe.wait_ge(lo_split, c + 1)
                for t in range(TT):
                    if wait_bank is not None and q == 0:
                        pe.wait_ge(main_free, wait_bank + t)
                    for kk in range(2):
                        k = 2 * q + kk
                        if wait_tiles and t == 0:
                            pe.wait_ge(hn_lo, KT * n + k + 1)
                        rows_ = slice(t * P, (t + 1) * P)
                        cols_ = slice(kk * 512, (kk + 1) * 512)
                        start, stop = k == 0, k == KT - 1
                        pe.matmul(ps[:, t, :], hn_h[:, k, rows_], w_h[:, q, cols_], start=start, stop=False)
                        pe.matmul(ps[:, t, :], hn_h[:, k, rows_], w_l[:, q, cols_], start=False, stop=False)
                        m = pe.matmul(ps[:, t, :], hn_l[:, k, rows_], w_h[:, q, cols_], start=False, stop=stop)
                    if t == TT - 1:
                        m.then_inc(chunk_used, 1)
                    elif q == 3:
                        m.then_inc(full, 1)

            def project(base, a_base, chunks, tiles, slot0, ready, r_base, per_tile):
                per = {3: 4, 2: 2, 1: 4}[chunks]

                def body(i, first, last):
                    for dd in range(per):
                        d = i * per + dd
                        a = a_base + d
                        pe.wait_ge(out_free, a - 1)
                        for part in range(chunks):
                            c = base + (i * per + dd) * chunks + part
                            slot = (dd * chunks + part) % RING
                            pe.wait_ge(lo_split, c + 1)
                            for k in range(8 * part, min(8 * part + 8, tiles)):
                                if first and dd == 0:
                                    pe.wait_ge(ready, r_base + per_tile * (k + 1))
                                b = operand_blocks(k % 8)
                                m = mm3(ps[:, 4 + dd % 2, :], w_h[:, slot, b], w_l[:, slot, b],
                                        act_h[:, slot0 + k, :], act_l[:, slot0 + k, :],
                                        k == 0, k == tiles - 1)
                            m.then_inc(chunk_used, 1)

                rolled(pe, KT // per, body)

            def ffn_up(n, base, g_base):
                def body(i, first, last):
                    for k in range(4):
                        pe.wait_ge(main_free, g_base + 4 * i + k - 3)
                        tile_chunk(base + 4 * i + k, k, k, n, first and k == 0)
                        if first and k == 0:
                            norm_sums(n)
                        if first and k == 1:
                            norm_row(n)

                rolled(pe, PAIRS // 2, body)

            pe.wait_ge(rel_landed, 16 * 3)
            pe.matmul(ps[0:HEADS, 6, 0:384], rel_sb, onehot_sb, start=True, stop=True).then_inc(lines_summed, 1)
            pe.wait_ge(consts_ready, 3)

            def v_block(j, first, last):
                for q in range(4):
                    token_chunk(C_V + 4 * j + q, q, v_full, None if first else G_V + 4 * j - 3, first, 0)

            def v_first():
                for q in range(4):
                    token_chunk(C_V + q, q, v_full, None, True, 0)
                    if q == 1:
                        norm_sums(0)
                    if q == 2:
                        norm_row(0)

            v_first()
            with pe.Fori(1, 4) as j:
                v_block(j, False, False)

            def spatial(g):
                pe.wait_ge(wr_lo, g + 1)
                if g >= 2:
                    pe.wait_ge(out_free, A_S + g - 1)
                for c in range(TT):
                    t = slice(c * P, (c + 1) * P)
                    m = mm3(ps[:, 4 + g % 2, t], act_h[:, g, t], act_l[:, g, t],
                            act_h[:, 16 + g % 2, t], act_l[:, 16 + g % 2, t], True, True)
                m.then_inc(mix_full, 1)

            pe.wait_ge(v_hi, 16)
            for g in range(GROUPS):
                pe.wait_ge(main_free, G_U + g - 3)
                tile_chunk(C_U + g, g % 4, g % 4, 0, False)
                if g == 1:
                    pe.wait_ge(v_lo, 16)
                if g >= 1:
                    spatial(g - 1)
            spatial(GROUPS - 1)
            project(C_OUT, A_OUT, 2, GROUPS, 0, gated_lo, 0, 1)
            ffn_up(1, C_UP0, G_UP0)
            project(C_DN0, A_DN0, 3, PAIRS, 0, prod_lo, 0, 1)

            for q in range(4):
                token_chunk(C_KV + q, q, kv_full, G_KV - 3, True, 2)
                if q == 0:
                    norm_sums(2)
                if q == 1:
                    norm_row(2)

            pe.wait_ge(halves_ready, 3)

            def q_sums(i):
                pe.wait_ge(q_squared, i + 1)
                for t in range(TT):
                    m = pe.matmul(ps[:, MISC, i * 8 + 2 * t:i * 8 + 2 * t + 2],
                                  q_sq[:, i % 2, t * P:(t + 1) * P], halves[:], start=True, stop=True)
                m.then_inc(q_summed, 1)

            for i in range(KT):
                pe.wait_ge(main_free, G_Q + i - 3)
                tile_chunk(C_Q + i, i % 4, i % 4, 2, False)
                if i >= 1:
                    if i == 1:
                        pe.wait_ge(row_ready, 3)
                    q_sums(i - 1)
                if i == 1:
                    for c in range(2):
                        for t in range(TT):
                            pe.wait_ge(k_normed, t + 1)
                            pe.transpose(ps[:, 5 + c, t * P:(t + 1) * P], k_n[:, t, c * P:(c + 1) * P],
                                         ident[:]).then_inc(k_turned, 1)
            q_sums(KT - 1)

            def attend(u):
                if u < UNITS:
                    c, n, i = u // 16, (u // 4) % TT, u % 4
                    if u == 0:
                        pe.wait_ge(kt_lo, 2)
                        pe.wait_ge(main_free, G_Q + KT)
                    if u >= 2:
                        pe.wait_ge(s_biased, 2 * u - 2)
                    first_key = P if n == 0 else 0
                    keys = slice((n - 1) * P + first_key, (n + 1) * P)
                    q = slice(n * P, (n + 1) * P)
                    for x in range(2):
                        part = slice(x * HD, (x + 1) * HD)
                        m = mm3(ps[:, x + 2 * (u % 2), first_key:256],
                                act_h[part, SLOT_Q + 4 * c + i, q], act_l[part, SLOT_Q + 4 * c + i, q],
                                act_h[part, SLOT_K + c, keys], act_l[part, SLOT_K + c, keys], True, True)
                    m.then_inc(s_full, 1)
                if 1 <= u < UNITS + 1:
                    w = u - 1
                    pe.wait_ge(p_scaled, 2 * w + 2)
                    if w >= 2:
                        pe.wait_ge(p_lo, w - 1)
                    for half in range(1 if (w // 4) % TT == 0 else 0, 2):
                        for x in range(2):
                            m = pe.transpose(ps[:, 4 + w % 2, (2 * half + x) * P:(2 * half + x + 1) * P],
                                             at_s[:, w % 2, x, half * P:(half + 1) * P], ident[:])
                    m.then_inc(p_turned, 1)
                if 3 <= u:
                    w = u - 3
                    c, n = w // 16, (w // 4) % TT
                    pe.wait_ge(p_lo, w + 1)
                    if w == 0:
                        pe.wait_ge(vv_lo, TT)
                    if w >= 2:
                        pe.wait_ge(o_lo, 2 * w - 2)
                    halves_ = [1] if n == 0 else [0, 1]
                    for half in halves_:
                        t = n - 1 + half
                        v = slice(t * 256 + c * P, t * 256 + (c + 1) * P)
                        pt = slice(half * 256, (half + 1) * 256)
                        m = mm3(ps[:, 6 + w % 2, 0:256], v_h[:, v], v_l[:, v],
                                act_h[:, SLOT_P + w % 2, pt], act_l[:, SLOT_P + w % 2, pt],
                                half == halves_[0], half == 1)
                    m.then_inc(o_full, 1)

            for u in range(UNITS + 3):
                attend(u)
            project(C_WO, A_WO, 1, KT, SLOT_O, o_lo, 2 * UNITS, 0)
            ffn_up(3, C_UP1, G_UP1)
            project(C_DN1, A_DN1, 3, PAIRS, 0, prod_lo, PAIRS, 1)


def bucket_of_distance():
    n = np.arange(MAX_DIST)
    exact = BUCKETS // 2
    large = exact + (np.log(np.maximum(n, 1).astype(np.float32) / exact)
                     / math.log(MAX_DIST / exact) * (BUCKETS - exact)).astype(np.int32)
    return np.where(n < exact, n, np.minimum(large, BUCKETS - 1))


def constants():
    onehot = np.zeros((BUCKETS, 384), np.float32)
    masked = np.full((HEADS, 384), MASKED, np.float32)
    for dist, b in enumerate(bucket_of_distance()):
        onehot[b, 255 - dist] = 1.0
        masked[:, 255 - dist] = 0.0
    return onehot, masked


def kernel(**inputs):
    import concourse.bacc as bacc
    from concourse.bass_utils import run_bass_kernel_spmd

    a = {k: np.asarray(v) for k, v in inputs.items()}

    def by_tile(w):
        k, n = w.shape
        blocks = w.reshape(k // P, P, n // P, P).transpose(2, 1, 0, 3)
        parts = []
        for tile in blocks:
            for lo in range(0, k // P, 8):
                part = tile[:, lo:lo + 8].reshape(P, -1)
                parts.append(np.pad(part, ((0, 0), (0, CHUNK - part.shape[1]))))
        return np.stack(parts)

    def by_token(w):
        n = w.shape[1]
        return w.reshape(4, 2, P, n // 512, 512).transpose(3, 0, 2, 1, 4).reshape(-1, P, CHUNK)

    def pairs(w, axis):
        w = np.moveaxis(w, axis, -1)
        w = w.reshape(w.shape[:-1] + (2, PAIRS, P))
        w = np.swapaxes(w, -3, -2)
        return np.moveaxis(w.reshape(w.shape[:-3] + (2 * PAIRS * P,)), -1, axis)

    heads = np.arange(HEADS).reshape(2, 2, 4).transpose(0, 2, 1).reshape(-1)
    w_in = a["sgu_w_in"][0]
    w_qkv = a["attn_w_qkv"][0]
    w_q = w_qkv[:, :D_MODEL].reshape(D_MODEL, HEADS, HD)[:, heads].reshape(D_MODEL, D_MODEL)
    w_o = a["attn_w_o"][0].reshape(HEADS, HD, D_MODEL)[heads].reshape(D_MODEL, D_MODEL)
    stream = np.concatenate([
        by_token(w_in[:, 2 * D_MODEL:]), by_tile(w_in[:, :2 * D_MODEL]), by_tile(a["sgu_w_out"][0]),
        by_tile(pairs(a["ffn_w_up"][0], 1)), by_tile(a["ffn_w_down"][0]),
        by_token(w_qkv[:, D_MODEL:]), by_tile(w_q), by_tile(w_o),
        by_tile(pairs(a["ffn_w_up"][1], 1)), by_tile(a["ffn_w_down"][1])])
    down = lambda v: v.reshape(-1, P).T
    conv = [np.stack([*pairs(a["ffn_conv_w"][i], 1), pairs(a["ffn_conv_b"][i], 0)], -1)
            .reshape(2 * PAIRS, P, 4).transpose(1, 0, 2).reshape(P, -1) for i in range(2)]
    cols = np.concatenate([down(a["mix_norm"]), down(a["ffn_norm"]), down(a["sgu_v_gain"][0]), *conv], 1)
    rows = np.concatenate([a["attn_q_gain"][0], a["attn_k_gain"][0], a["attn_sinks"][0][heads]])
    onehot, masked = constants()
    arrays = {
        "x_t": a["x"][0].T.reshape(KT, P, SEQ),
        "stream": stream,
        "cols": cols,
        "rows": rows,
        "ws_t": a["sgu_w_s"][0].transpose(0, 2, 1),
        "b_s": a["sgu_b_s"][0],
        "rel": a["rel_bias"][:, heads],
        "onehot": onehot,
        "masked": masked,
    }
    arrays = {k: np.ascontiguousarray(v) for k, v in arrays.items()}
    nc = bacc.Bacc("TRN2", target_bir_lowering=False, num_devices=1)
    args = [nc.dram_tensor(k, v.shape, F32, kind="ExternalInput").ap() for k, v in arrays.items()]
    args.append(nc.dram_tensor("out_t", (KT, P, SEQ), F32, kind="ExternalOutput").ap())
    build(nc, *args)
    r = run_bass_kernel_spmd(nc, [arrays], core_ids=[0])
    return np.ascontiguousarray(r.results[0]["out_t"].reshape(D_MODEL, SEQ).T)[None]
```

```python
import math
from contextlib import ExitStack

import numpy as np

import concourse.bass as bass
from concourse import mybir

F32 = mybir.dt.float32
F32R = mybir.dt.float32r
ALU = mybir.AluOpType
ACT = mybir.ActivationFunctionType
AX_X = mybir.AxisListType.X

P = 128
D_MODEL = 1024
SEQ = 512
KT = D_MODEL // P
TT = SEQ // P
GROUPS = 16
HEADS = 16
KV_HEADS = 4
HD = 64
D_FF = 2816
PAIRS = D_FF // P
BUCKETS = 32
MAX_DIST = 128
EPS = 1e-6
MASKED = -1e30

CHUNK = 1024
C_V = 0
C_U = C_V + 16
C_OUT = C_U + 16
C_UP0 = C_OUT + 2 * KT
C_DN0 = C_UP0 + 2 * PAIRS
C_KV = C_DN0 + 3 * KT
C_Q = C_KV + 4
C_WO = C_Q + KT
C_UP1 = C_WO + KT
C_DN1 = C_UP1 + 2 * PAIRS
CHUNKS = C_DN1 + 3 * KT
RING = 4
RAW = 2
AHEAD = 3

G_V, G_U, G_UP0, G_KV, G_UP1 = 0, 16, 32, 76, 80
A_S, A_OUT, A_DN0, A_WO, A_DN1 = 0, 16, 24, 32, 40
MISC = 7
B_S, B_T, B_O, B_Q = 0, 2, 4, 6

PC_MIX, PC_FFN, PC_VG, PC_CONV = 0, 2 * KT, 4 * KT, 4 * KT + GROUPS
PC_ALL = PC_CONV + 2 * 2 * PAIRS * 4
PR_QG, PR_KG, PR_SINK, PR_ALL = 0, HD, 2 * HD, 2 * HD + HEADS

SLOT_Q, SLOT_K, SLOT_V, SLOT_P = 0, 8, 12, 15
P_RING = 4
S_RING = 3
UNITS = KT * TT
Q_EARLY = 3
WO_STEP = 24
STEPS = WO_STEP + 16
LAG_T, LAG_PV, LAG_O = 3, 5, 6


def rolled(eng, n, body):
    body(0, True, n == 1)
    if n > 3:
        with eng.Fori(1, n - 1) as i:
            body(i, False, False)
    else:
        for i in range(1, n - 1):
            body(i, False, False)
    if n > 1:
        body(n - 1, False, True)


def build(nc, x_t, stream, cols, rows, ws_t, b_s, rel, onehot, masked, out_t):
    ctx = ExitStack()
    with ctx:
        def sb(name, shape, dt=F32):
            return ctx.enter_context(nc.sbuf_tensor(name, shape, dt))

        def sem(name):
            return ctx.enter_context(nc.semaphore(name))

        ps = ctx.enter_context(nc.psum_tensor("ps", [P, 8, 512], F32))
        h = sb("h", [P, KT, SEQ])
        hn_h = sb("hn_h", [P, KT, SEQ], F32R)
        hn_l = sb("hn_l", [P, KT, SEQ], F32R)
        act_h = sb("act_h", [P, PAIRS, SEQ], F32R)
        act_l = sb("act_l", [P, PAIRS, SEQ], F32R)
        raw = sb("raw", [P, RAW, CHUNK])
        w_h = sb("w_h", [P, RING, CHUNK], F32R)
        w_l = sb("w_l", [P, RING, CHUNK], F32R)
        work = sb("work", [P, 5632])
        r_row = sb("r_row", [P, SEQ])
        ident = sb("ident", [P, P])
        ones = sb("ones", [P, P])
        halves = sb("halves", [P, 2])
        colp = sb("colp", [P, PC_ALL])
        rowp = sb("rowp", [P, PR_ALL])
        negsink = sb("negsink", [P, HEADS])
        qk_gain = sb("qk_gain", [P, HD])
        half_neg = sb("half_neg", [P, 64])
        mean = sb("mean", [P, 64])
        r_col = sb("r_col", [P, TT])
        r_v = sb("r_v", [P, TT])
        r2_col = sb("r2_col", [P, TT])
        r8_col = sb("r8_col", [P, TT])
        v_sq = sb("v_sq", [P, TT, 4])
        r_k = sb("r_k", [P, TT * KV_HEADS])
        r_q = sb("r_q", [P, 64])
        soft = sb("soft", [P, 6, 2 * UNITS])
        line_sb = sb("line_sb", [HEADS, 384])

        sq = work[:, 4608:5120]
        sq_sum = work[:, 5120:5632]
        diag = sq.rearrange("p (t q) -> p t q", t=TT)
        ff_a = work[:, 0:2 * 514].rearrange("p (r n) -> p r n", r=2)
        ff_c = work[:, 1028:1028 + 2048].rearrange("p (r n) -> p r n", r=4)
        ff_p = work[:, 3076:3076 + 1024].rearrange("p (r n) -> p r n", r=2)
        sg_a = work[:, 0:1024].rearrange("p (r n) -> p r n", r=2)
        sg_u = work[:, 1024:2048].rearrange("p (r n) -> p r n", r=2)
        sg_w = work[:, 2048:3072].rearrange("p (r n) -> p r n", r=2)
        sg_s = work[:, 3072:3584]
        ring_w = work[:, 3584:4096].rearrange("p (r n) -> p r n", r=4)
        ring_b = work[:, 4096:4608].rearrange("p (r n) -> p r n", r=4)
        at_bias = work[:, 0:4096].rearrange("p (g n) -> p g n", g=HEADS)
        at_s = work[:, 4096:5632].rearrange("p (r x n) -> p r x n", r=S_RING, x=2)
        kv = work[:, 0:2048].rearrange("p (t n) -> p t n", t=TT)
        kv_sq = work[:, 2048:2560].rearrange("p (r n) -> p r n", r=2)
        q_sq = r_row
        k_n = work[:, 3584:4608].rearrange("p (t n) -> p t n", t=TT)
        rel_sb = work[0:BUCKETS, 0:HEADS]
        onehot_sb = work[0:BUCKETS, 512:896]
        masked_sb = work[0:HEADS, 1024:1408]
        v_h = act_h[:, SLOT_V:SLOT_V + 3, :].rearrange("p s n -> p (s n)")
        v_l = act_l[:, SLOT_V:SLOT_V + 3, :].rearrange("p s n -> p (s n)")

        def v_parts(v, t):
            return v[:, t * 384:(t + 1) * 384].rearrange("p (c z d) -> p c z d", c=2, z=3)[:, :, 0:3:2, :]

        def v_zeros(v):
            return v.rearrange("p (m z d) -> p m z d", m=2 * TT, z=3)[:, :, 1, :]

        lines = nc.dram_tensor("rel_lines", (HEADS, P, 384), F32, kind="Internal").ap()

        params_landed = sem("params_landed")
        rows_landed = sem("rows_landed")
        rel_landed = sem("rel_landed")
        x_landed = [sem(f"x_landed{d}") for d in range(KT)]
        raw_landed = [sem(f"raw_landed{s}") for s in range(RAW)]
        ws_landed = [sem(f"ws_landed{s}") for s in range(4)]
        b_landed = [sem(f"b_landed{s}") for s in range(4)]
        lines_stored = sem("lines_stored")
        bias_landed = [sem(f"bias_landed{c}") for c in range(2)]
        out_stored = sem("out_stored")
        hi_split = sem("hi_split")
        lo_split = sem("lo_split")
        chunk_used = sem("chunk_used")
        main_free = sem("main_free")
        out_free = sem("out_free")
        consts_zeroed = sem("consts_zeroed")
        consts_ready = sem("consts_ready")
        halves_ready = sem("halves_ready")
        gains_ready = sem("gains_ready")
        lines_summed = sem("lines_summed")
        lines_ready = sem("lines_ready")
        pads_zeroed = sem("pads_zeroed")
        hn_hi = sem("hn_hi")
        hn_lo = sem("hn_lo")
        squared = sem("squared")
        sq_added = sem("sq_added")
        col_summed = sem("col_summed")
        mean_ready = sem("mean_ready")
        r_ready = sem("r_ready")
        diag_ready = sem("diag_ready")
        row_spread = sem("row_spread")
        row_ready = sem("row_ready")
        v_full = sem("v_full")
        v_gelu = sem("v_gelu")
        v_squared = sem("v_squared")
        v_hi = sem("v_hi")
        v_lo = sem("v_lo")
        v_sum = sem("v_sum")
        vmean_ready = sem("vmean_ready")
        rv_ready = sem("rv_ready")
        ws_masked = sem("ws_masked")
        wr_scaled = sem("wr_scaled")
        wr_hi = sem("wr_hi")
        wr_lo = sem("wr_lo")
        u_gelu = sem("u_gelu")
        mix_full = sem("mix_full")
        gated = sem("gated")
        gated_hi = sem("gated_hi")
        gated_lo = sem("gated_lo")
        conv_0 = sem("conv_0")
        conv_1 = sem("conv_1")
        conv_2 = sem("conv_2")
        silu_done = sem("silu_done")
        prod = sem("prod")
        prod_hi = sem("prod_hi")
        prod_lo = sem("prod_lo")
        kv_full = sem("kv_full")
        padded = sem("padded")
        vv_hi = sem("vv_hi")
        vv_lo = sem("vv_lo")
        k_squared = sem("k_squared")
        k_ss = sem("k_ss")
        k_mean = sem("k_mean")
        rk_ready = sem("rk_ready")
        k_scaled = sem("k_scaled")
        k_normed = sem("k_normed")
        k_turned = sem("k_turned")
        kt_hi = sem("kt_hi")
        kt_lo = sem("kt_lo")
        q_hi = sem("q_hi")
        q_squared = sem("q_squared")
        q_free = sem("q_free")
        wo_half = sem("wo_half")
        wo_added = sem("wo_added")
        wo_first = sem("wo_first")
        q_summed = sem("q_summed")
        rx_ready = sem("rx_ready")
        q_scaled = sem("q_scaled")
        q_mean = sem("q_mean")
        q_pow = sem("q_pow")
        rq_ready = sem("rq_ready")
        s_full = sem("s_full")
        s_biased = sem("s_biased")
        s_max = sem("s_max")
        m_ready = sem("m_ready")
        sink_off = sem("sink_off")
        p_exp = sem("p_exp")
        sink_exp = sem("sink_exp")
        den = sem("den")
        rden = sem("rden")
        p_scaled = sem("p_scaled")
        p_turned = sem("p_turned")
        p_hi = sem("p_hi")
        p_lo = sem("p_lo")
        o_full = sem("o_full")
        o_hi = sem("o_hi")
        o_lo = sem("o_lo")

        block = ctx.enter_context(nc.Block())

        def operand_blocks(kb):
            return slice(kb * P, (kb + 1) * P)

        def filler_chunk(u):
            if u % 4 or u >= STEPS or 4 * (KT - Q_EARLY) <= u < WO_STEP:
                return None
            return C_Q + Q_EARLY + u // 4 if u < WO_STEP else C_WO + (u - WO_STEP) // 4

        def unit(u):
            return 2 * (u // 8) + u % 2, 2 * (u // 4 % 2) + u % 4 // 2

        def quad(x, q):
            n = q % 2 * 2 * P
            return x[:, 2 * (q // 2):2 * (q // 2) + 2, n:n + 2 * P].rearrange("p i (n q) -> p i n q", n=2)

        def quad_bank(q):
            return ps[:, B_O + q % 2, :].rearrange("p (n i q) -> p i n q", n=2, i=2)

        def settle(eng):
            eng.wait_ge(params_landed, 16)

        @block.sync
        def _(sp):
            def load(c, slot, again):
                if again:
                    sp.wait_ge(lo_split, c - RAW + 1)
                sp.dma_start(raw[:, slot, :], stream[c]).then_inc(raw_landed[slot], 16)

            sp.dma_start(colp[:], cols).then_inc(params_landed, 16)
            for d in range(KT):
                sp.dma_start(h[:, d, :], x_t[d]).then_inc(x_landed[d], 16)
                if d % 2 == 1 and d < 2 * RAW:
                    load(d // 2, d // 2, False)
            sp.dma_start(rowp[:], rows.partition_broadcast(P)).then_inc(rows_landed, 16)
            with sp.Fori(1, CHUNKS // RAW) as i:
                for k in range(RAW):
                    load(RAW * i + k, k, True)
            for d in range(KT):
                sp.wait_ge(out_free, A_DN1 + d + 1)
                sp.dma_start(out_t[d], h[:, d, :]).then_inc(out_stored, 16)
            sp.wait_ge(out_stored, 16 * KT)

        @block.gpsimd
        def _(pool):
            pool.memset(ident[:], 0.0).then_inc(consts_zeroed, 1)
            pool.wait_ge(consts_zeroed, 1)
            pool.affine_select(out=ident[:], in_=ident[:], compare_op=ALU.not_equal, fill=1.0, base=0,
                               pattern=[[-1, P]], channel_multiplier=1).then_inc(consts_ready, 1)
            pool.memset(ones[:], 1.0).then_inc(consts_ready, 1)
            pool.memset(half_neg[:], -0.5).then_inc(consts_ready, 1)
            pool.wait_ge(consts_ready, 3)

            pool.dma_start(rel_sb, rel).then_inc(rel_landed, 16)
            pool.dma_start(onehot_sb, onehot).then_inc(rel_landed, 16)
            pool.dma_start(masked_sb, masked).then_inc(rel_landed, 16)

            def root(n_sem, n, dst, width, done):
                pool.wait_ge(n_sem, n)
                pool.tensor_tensor(dst, mean[:, 0:width], half_neg[:, 0:width], ALU.pow)\
                    .then_inc(done, 1)

            root(mean_ready, 1, r_col[:], TT, r_ready)

            def fetch(g, s, again):
                if again:
                    pool.wait_ge(wr_scaled, g - 3)
                    pool.wait_ge(out_free, A_S + g - 3)
                pool.dma_start(ring_w[:, s, :], ws_t[g]).then_inc(ws_landed[s], 16)
                pool.dma_start(ring_b[:, s, :], b_s[g].partition_broadcast(P)).then_inc(b_landed[s], 16)

            def mask(g, s, turn):
                pool.wait_ge(ws_landed[s], 16 * (turn + 1))
                settle(pool)
                pool.affine_select(out=ring_w[:, s, :], in_=ring_w[:, s, :], compare_op=ALU.is_ge, fill=0.0,
                                   base=0, pattern=[[1, P]], channel_multiplier=-1).then_inc(ws_masked, 1)

            for g in range(4):
                fetch(g, g, False)
            for g in range(4):
                mask(g, g, 0)
            root(vmean_ready, 1, r_v[:], TT, rv_ready)
            pool.wait_ge(lines_ready, 1)
            pool.dma_start(lines, line_sb[:].unsqueeze(1).broadcast_to([HEADS, P, 384]))\
                .then_inc(lines_stored, 16)
            for i in range(1, GROUPS // 4):
                for s in range(4):
                    fetch(4 * i + s, s, True)
                    mask(4 * i + s, s, i)
            root(mean_ready, 2, r_col[:], TT, r_ready)
            root(mean_ready, 3, r_col[:], TT, r_ready)
            pool.wait_ge(chunk_used, C_KV)
            pool.wait_ge(r_ready, 3)
            pads = [act[rows_, SLOT_K + x:SLOT_K + 4:2, :] for act in (act_h, act_l)
                    for x, rows_ in ((0, slice(HD, P)), (1, slice(0, HD)))]
            for i, part in enumerate([*pads, v_zeros(v_h), v_zeros(v_l)]):
                pool.memset(part.bitcast(F32), 0.0).then_inc(padded, 1)
                pool.wait_ge(padded, i + 1)
            root(k_mean, 1, r_k[:], TT * KV_HEADS, rk_ready)

            def q_root(j):
                part = slice(8 * j, 8 * j + 8)
                pool.wait_ge(q_mean, j + 1)
                pool.tensor_tensor(r_q[:, part], mean[:, part], half_neg[:, part], ALU.pow).then_inc(q_pow, 1)

            q_root(0)
            q_root(1)
            pool.wait_ge(lo_split, C_Q + Q_EARLY + AHEAD)
            for u in range(STEPS):
                if u % 4 == 2 and u // 4 + 2 < KT:
                    q_root(u // 4 + 2)
                if 1 <= u < UNITS + 1:
                    w = u - 1
                    first_key = P if unit(w)[1] == 0 else 0
                    pool.wait_ge(rden, w + 1)
                    for x in range(2):
                        part = at_s[:, w % S_RING, x, first_key:]
                        pool.tensor_scalar(part, part, soft[:, 5, 2 * w + x:2 * w + x + 1], 1.0, ALU.mult,
                                           ALU.mult).then_inc(p_scaled, 1)
                if filler_chunk(u) is not None:
                    c = filler_chunk(u) + AHEAD
                    pool.wait_ge(hi_split, c + 1)
                    pool.tensor_tensor(w_l[:, c % RING, :], raw[:, c % RAW, :], w_h[:, c % RING, :].bitcast(F32),
                                       ALU.subtract).then_inc(lo_split, 1)
            root(mean_ready, 4, r_col[:], TT, r_ready)

        @block.scalar
        def _(act):
            def tick(c, slot):
                if isinstance(c, int) and c + AHEAD >= CHUNKS:
                    return
                split(c + AHEAD, (slot + AHEAD) % RING, True)

            def split(c, slot, again):
                act.wait_ge(raw_landed[slot % RAW], 16 * (c // RAW + 1) if isinstance(c, int)
                            else (c - slot % RAW) * (16 // RAW) + 16)
                if again and not (isinstance(c, int) and c < RING):
                    act.wait_ge(chunk_used, c - RING + 1)
                act.activation(w_h[:, slot, :], raw[:, slot % RAW, :], ACT.Copy).then_inc(hi_split, 1)

            def spread_hi(n, d, gain, ready, count, first):
                if not first:
                    act.wait_ge(sq_added, KT * n + d)
                act.wait_ge(ready, count)
                settle(act)
                act.activation(hn_h[:, d, :], h[:, d, :], ACT.Copy, scale=gain).then_inc(hn_hi, 1)
                act.activation(sq, h[:, d, :], ACT.Square).then_inc(squared, 1)

            def project(n, base, a_base, chunks, gain_col):
                per = {3: 4, 2: 2, 1: 4}[chunks]

                def body(i, first, last):
                    for dd in range(per):
                        d = i * per + dd
                        for k in range(chunks):
                            tick(base + (i * per + dd) * chunks + k, (dd * chunks + k) % RING)
                        if n < 4:
                            spread_hi(n, d, colp[:, gain_col + d:gain_col + d + 1] if isinstance(d, int)
                                      else colp[:, bass.ds(gain_col + d, 1)], out_free, a_base + d + 1,
                                      first and dd == 0)

                rolled(act, KT // per, body)

            def ffn(layer, base, g_base):
                def body(i, first, last):
                    for k in range(4):
                        tile = 4 * i + k
                        g = g_base + tile
                        n = 44 * layer + tile
                        pair = PAIRS * layer + 2 * i + k // 2
                        if k % 2 == 0 and not (first and k == 0):
                            pp = 2 * i + k // 2 - 1
                            act.wait_ge(prod, pair)
                            settle(act)
                            act.activation(act_h[:, pp, :], ff_p[:, (k // 2 + 1) % 2, :], ACT.Copy)\
                                .then_inc(prod_hi, 1)
                        if not (first and k < 2):
                            tick(base + tile, k)
                        if k % 2 == 1:
                            act.wait_ge(conv_2, n)
                            act.activation(ff_c[:, k - 1, :], ff_c[:, k - 1, :], ACT.Silu)\
                                .then_inc(silu_done, 1)
                        act.wait_ge(main_free, g + 1)
                        if not (first and layer == 0):
                            act.wait_ge(prod, pair - 1)
                        settle(act)
                        pc = PC_CONV + 4 * (44 * layer + tile)
                        act.activation(ff_c[:, k, :], ff_a[:, k % 2, 2:514], ACT.Identity,
                                       bias=colp[:, bass.ds(pc + 3, 1)], scale=colp[:, bass.ds(pc + 2, 1)])\
                            .then_inc(conv_0, 1)

                tick(base, 0)
                tick(base + 1, 1)
                rolled(act, PAIRS // 2, body)
                act.wait_ge(prod, PAIRS * (layer + 1))
                act.activation(act_h[:, PAIRS - 1, :], ff_p[:, 1, :], ACT.Copy).then_inc(prod_hi, 1)

            act.wait_ge(params_landed, 16)
            for d in range(KT):
                act.wait_ge(x_landed[d], 16)
                act.activation(hn_h[:, d, :], h[:, d, :], ACT.Copy, scale=colp[:, PC_MIX + d:PC_MIX + d + 1])\
                    .then_inc(hn_hi, 1)
                if d in (1, 3, 5):
                    split(d // 2, d // 2, False)
            for d in range(KT):
                if d >= 1:
                    act.wait_ge(sq_added, d)
                act.activation(sq, h[:, d, :], ACT.Square).then_inc(squared, 1)

            def v_block(j, first, last):
                for q in range(4):
                    tick(C_V + 4 * j + q, q)
                for t in range(TT):
                    u = 4 * j + t
                    act.wait_ge(main_free, G_V + u + 1)
                    if not (first and t < 2):
                        act.wait_ge(v_lo, u - 1)
                    act.activation(sg_u[:, t % 2, :], sg_a[:, t % 2, :], ACT.Gelu).then_inc(v_gelu, 1)
                    act.wait_ge(v_gelu, u + 1)
                    settle(act)
                    act.activation(sg_w[:, 0, :], sg_u[:, t % 2, :], ACT.Square,
                                   accum_out=v_sq[:, t, bass.ds(j, 1)]).then_inc(v_squared, 1)
                    act.activation(act_h[:, bass.ds(4 * j, 4), t * P:(t + 1) * P],
                                   sg_u[:, t % 2, :].rearrange("p (g d) -> p g d", g=4), ACT.Copy)\
                        .then_inc(v_hi, 1)
                    act.wait_ge(v_squared, u + 1)

            rolled(act, 4, v_block)

            def wr_part(g, par):
                act.wait_ge(wr_scaled, g + 1)
                if not (isinstance(g, int) and g < 2):
                    act.wait_ge(mix_full, g - 1)
                act.activation(act_h[:, 16 + par, :], sg_w[:, par, :], ACT.Copy).then_inc(wr_hi, 1)

            def gate_hi(g):
                act.wait_ge(gated, g + 1)
                settle(act)
                act.activation(act_h[:, g, :], sg_s, ACT.Copy).then_inc(gated_hi, 1)

            wr_part(0, 0)

            def u_block(i, first, last):
                for k in range(4):
                    g = 4 * i + k
                    tick(C_U + g, k)
                    act.wait_ge(main_free, G_U + g + 1)
                    if not (first and k < 2):
                        act.wait_ge(gated, g - 1)
                    act.activation(sg_u[:, k % 2, :], sg_a[:, k % 2, :], ACT.Gelu).then_inc(u_gelu, 1)
                    if not (last and k == 3):
                        wr_part(g + 1, (k + 1) % 2)
                    if not (first and k == 0):
                        gate_hi(g - 1)

            rolled(act, GROUPS // 4, u_block)
            gate_hi(GROUPS - 1)
            project(1, C_OUT, A_OUT, 2, PC_FFN)
            ffn(0, C_UP0, G_UP0)
            project(2, C_DN0, A_DN0, 3, PC_MIX + KT)

            for q in range(4):
                tick(C_KV + q, q)
            act.wait_ge(padded, 6)
            for t in range(TT):
                act.wait_ge(main_free, G_KV + t + 1)
                act.activation(v_parts(v_h, t), kv[:, t, 256:512].rearrange("p (c x d) -> p c x d", c=2, x=2),
                               ACT.Copy).then_inc(vv_hi, 1)
                if t >= 2:
                    act.wait_ge(k_ss, t - 1)
                act.activation(kv_sq[:, t % 2, :], kv[:, t, 0:256], ACT.Square).then_inc(k_squared, 1)

            def q_part(j):
                act.wait_ge(chunk_used, C_Q + j + 1)
                act.activation(act_h[:, SLOT_Q + j, :], ps[:, B_Q + j % 2, :], ACT.Copy).then_inc(q_hi, 1)
                if j >= 1:
                    act.wait_ge(q_summed, j)
                act.activation(q_sq[:], ps[:, B_Q + j % 2, :], ACT.Square).then_inc(q_squared, 1)

            def load_bias(c):
                heads = slice(8 * c, 8 * c + 8)
                act.dma_start(at_bias[:, heads, :],
                              bass.AP(lines.tensor, P - 1 + c * 8 * P * 384, [[383, P], [P * 384, 8], [1, 256]]))\
                    .then_inc(bias_landed[c], 16)

            tick(C_Q, 0)
            q_part(0)
            tick(C_Q + 1, 1)
            q_part(1)
            act.wait_ge(lines_stored, 16)
            act.wait_ge(vv_lo, TT)
            act.wait_ge(k_normed, TT)
            load_bias(0)
            for c in range(2):
                act.wait_ge(k_turned, 4 * c + 4)
                for x in range(2):
                    part = slice(x * HD, (x + 1) * HD)
                    act.activation(act_h[part, SLOT_K + 2 * c + x, :], ps[part, B_O + c, :], ACT.Copy)\
                        .then_inc(kt_hi, 1)
            load_bias(1)
            tick(C_Q + 2, 2)

            def attend(u):
                if filler_chunk(u) is not None:
                    tick(filler_chunk(u), filler_chunk(u) % RING)
                if u % 4 == 0 and u // 4 + 2 < KT:
                    q_part(u // 4 + 2)
                w = u - LAG_T
                if 0 <= w < UNITS:
                    first_half = 256 if unit(w)[1] == 0 else 0
                    act.wait_ge(p_turned, w + 1)
                    if w >= P_RING:
                        act.wait_ge(o_full, (w - P_RING) // 2 + 1)
                    act.activation(act_h[:, SLOT_P + w % P_RING, first_half:], ps[:, B_T + w % 2, first_half:],
                                   ACT.Copy).then_inc(p_hi, 1)
                if u < UNITS:
                    first_key = P if unit(u)[1] == 0 else 0
                    act.wait_ge(sink_off, u + 1)
                    for x in range(2):
                        s = at_s[:, u % S_RING, x, first_key:]
                        act.activation(s, s, ACT.Exp, bias=soft[:, 0, 2 * u + x:2 * u + x + 1],
                                       accum_out=soft[:, 2, 2 * u + x:2 * u + x + 1]).then_inc(p_exp, 1)
                    act.activation(soft[:, 3, 2 * u:2 * u + 2], soft[:, 1, 2 * u:2 * u + 2], ACT.Exp)\
                        .then_inc(sink_exp, 1)
                w = u - LAG_O
                if w % 4 == 3 and 0 <= w < UNITS:
                    act.wait_ge(o_full, w // 2 + 1)
                    act.activation(quad(act_h, w // 4), quad_bank(w // 4), ACT.Copy).then_inc(o_hi, 1)

            for u in range(STEPS):
                attend(u)
            for j in range(KT // 2):
                tick(C_WO + 4 + j, j)
                for d in (2 * j, 2 * j + 1):
                    spread_hi(3, d, colp[:, PC_FFN + KT + d:PC_FFN + KT + d + 1], out_free, A_WO + d + 1, d == 0)
            ffn(1, C_UP1, G_UP1)
            project(4, C_DN1, A_DN1, 3, 0)

        @block.vector
        def _(dve):
            def tick(c, slot):
                if isinstance(c, int) and c + AHEAD >= CHUNKS:
                    return
                split(c + AHEAD, (slot + AHEAD) % RING)

            def split(c, slot):
                dve.wait_ge(hi_split, c + 1)
                dve.tensor_tensor(w_l[:, slot, :], raw[:, slot % RAW, :], w_h[:, slot, :].bitcast(F32),
                                  ALU.subtract).then_inc(lo_split, 1)

            def gain_lo(n, d, gain):
                dve.wait_ge(hn_hi, KT * n + d + 1)
                dve.scalar_tensor_tensor(out=hn_l[:, d, :], in0=h[:, d, :], scalar=gain,
                                         in1=hn_h[:, d, :].bitcast(F32), op0=ALU.mult, op1=ALU.subtract)\
                    .then_inc(hn_lo, 1)

            def add_squares(n, d, first):
                dve.wait_ge(squared, KT * n + d + 1)
                if first:
                    dve.tensor_copy(sq_sum, sq).then_inc(sq_added, 1)
                else:
                    dve.wait_ge(sq_added, KT * n + d)
                    dve.tensor_tensor(sq_sum, sq_sum, sq, ALU.add).then_inc(sq_added, 1)

            def spread_lo(n, d, gain, first):
                gain_lo(n, d, gain)
                add_squares(n, d, first)

            def finish_norm(n, c, row):
                tick(c, 0)
                dve.wait_ge(col_summed, n + 1)
                dve.tensor_scalar(mean[:, 0:TT], ps[:, MISC, 0:TT], 1.0 / D_MODEL, EPS, ALU.mult, ALU.add)\
                    .then_inc(mean_ready, 1)
                dve.wait_ge(r_ready, n + 1)
                if row is None:
                    return
                dve.tensor_tensor(diag, ident[:].unsqueeze(1).broadcast_to([P, TT, P]),
                                  r_col[:].unsqueeze(2).broadcast_to([P, TT, P]), ALU.mult)\
                    .then_inc(diag_ready, 1)
                tick(c + 1, 1)
                dve.wait_ge(row_spread, row + 1)
                dve.tensor_copy(r_row[:], ps[:, MISC, :]).then_inc(row_ready, 1)
                dve.wait_ge(row_ready, row + 1)

            def project(n, base, a_base, chunks, gain_col):
                per = {3: 4, 2: 2, 1: 4}[chunks]

                def body(i, first, last):
                    for dd in range(per):
                        d = i * per + dd
                        for k in range(chunks):
                            tick(base + (i * per + dd) * chunks + k, (dd * chunks + k) % RING)
                        dve.wait_ge(chunk_used, base + (d + 1) * chunks)
                        dve.tensor_tensor(h[:, d, :], ps[:, 4 + dd % 2, :], h[:, d, :], ALU.add)\
                            .then_inc(out_free, 1)
                        if n < 4:
                            dve.wait_ge(out_free, a_base + d + 1)
                            spread_lo(n, d, colp[:, bass.ds(gain_col + d, 1)], first and dd == 0)

                rolled(dve, KT // per, body)

            def ffn(layer, base, g_base):
                def product_lo(pair, pp, par):
                    dve.wait_ge(prod_hi, pair + 1)
                    dve.tensor_tensor(act_l[:, pp, :], ff_p[:, par, :], act_h[:, pp, :].bitcast(F32),
                                      ALU.subtract).then_inc(prod_lo, 1)

                def body(i, first, last):
                    for k in range(4):
                        tile = 4 * i + k
                        n = 44 * layer + tile
                        pair = PAIRS * layer + 2 * i + k // 2
                        pc = PC_CONV + 4 * (44 * layer + tile)
                        dve.wait_ge(chunk_used, base + tile + 1)
                        if not (first and layer == 0 and k < 2):
                            dve.wait_ge(conv_0, n - 1)
                        dve.tensor_tensor(ff_a[:, k % 2, 2:514], ps[:, k, :], r_row[:], ALU.mult)\
                            .then_inc(main_free, 1)
                        if k % 2 == 0 and not (first and k == 0):
                            product_lo(pair - 1, 2 * i + k // 2 - 1, (k // 2 + 1) % 2)
                        if not (first and k < 2):
                            tick(base + tile, k)
                        dve.wait_ge(conv_0, n + 1)
                        dve.scalar_tensor_tensor(out=ff_c[:, k, :], in0=ff_a[:, k % 2, 1:513],
                                                 scalar=colp[:, bass.ds(pc + 1, 1)], in1=ff_c[:, k, :],
                                                 op0=ALU.mult, op1=ALU.add).then_inc(conv_1, 1)
                        dve.wait_ge(conv_1, n + 1)
                        dve.scalar_tensor_tensor(out=ff_c[:, k, :], in0=ff_a[:, k % 2, 0:512],
                                                 scalar=colp[:, bass.ds(pc, 1)], in1=ff_c[:, k, :],
                                                 op0=ALU.mult, op1=ALU.add).then_inc(conv_2, 1)
                        if k % 2 == 1:
                            dve.wait_ge(silu_done, pair + 1)
                            dve.wait_ge(conv_2, n + 1)
                            dve.tensor_tensor(ff_p[:, k // 2, :], ff_c[:, k - 1, :], ff_c[:, k, :],
                                              ALU.mult).then_inc(prod, 1)

                finish_norm(2 * layer + 1, base, layer + 1)
                dve.memset(ff_a[:, :, 0:2], 0.0).then_inc(pads_zeroed, 1)
                dve.wait_ge(pads_zeroed, layer + 1)
                rolled(dve, PAIRS // 2, body)
                product_lo(PAIRS * (layer + 1) - 1, PAIRS - 1, 1)

            dve.memset(halves[:], 0.0).then_inc(halves_ready, 1)
            dve.wait_ge(halves_ready, 1)
            dve.memset(halves[0:HD, 0:1], 1.0).then_inc(halves_ready, 1)
            dve.memset(halves[HD:P, 1:2], 1.0).then_inc(halves_ready, 1)
            dve.wait_ge(params_landed, 16)
            for d in range(KT):
                dve.wait_ge(x_landed[d], 16)
                gain_lo(0, d, colp[:, PC_MIX + d:PC_MIX + d + 1])
                if d in (1, 3, 5):
                    split(d // 2, d // 2)
            for d in range(KT):
                add_squares(0, d, d == 0)
            dve.wait_ge(rows_landed, 16)
            dve.tensor_scalar(negsink[:], rowp[:, PR_SINK:PR_ALL], -1.0, None, ALU.mult)\
                .then_inc(gains_ready, 1)
            dve.tensor_tensor(qk_gain[:], rowp[:, PR_QG:PR_QG + HD], rowp[:, PR_KG:PR_KG + HD], ALU.mult)\
                .then_inc(gains_ready, 1)
            dve.wait_ge(lines_summed, 1)
            dve.tensor_tensor(line_sb[:], ps[0:HEADS, 6, 0:384], masked_sb, ALU.add).then_inc(lines_ready, 1)
            finish_norm(0, C_V, 0)

            def v_lo_part(j, t):
                u = 4 * j + t
                dve.wait_ge(v_hi, u + 1)
                dve.tensor_tensor(act_l[:, bass.ds(4 * j, 4), t * P:(t + 1) * P],
                                  sg_u[:, t % 2, :].rearrange("p (g d) -> p g d", g=4),
                                  act_h[:, bass.ds(4 * j, 4), t * P:(t + 1) * P].bitcast(F32),
                                  ALU.subtract).then_inc(v_lo, 1)

            def v_block(j, first, last):
                for q in range(4):
                    if not (first and q < 2):
                        tick(C_V + 4 * j + q, q)
                for t in range(TT):
                    u = 4 * j + t
                    if t < TT - 1:
                        dve.wait_ge(v_full, 3 * j + t + 1)
                    else:
                        dve.wait_ge(chunk_used, C_V + 4 * j + 4)
                    if not (first and t < 2):
                        dve.wait_ge(v_gelu, u - 1)
                    dve.tensor_scalar(sg_a[:, t % 2, :], ps[:, t, :], r_col[:, t:t + 1], None, ALU.mult)\
                        .then_inc(main_free, 1)
                    if t >= 1:
                        v_lo_part(j, t - 1)
                v_lo_part(j, TT - 1)

            rolled(dve, 4, v_block)

            dve.wait_ge(v_squared, 4 * TT)
            dve.tensor_reduce(mean[:, 8:8 + TT], v_sq[:], AX_X, ALU.add).then_inc(v_sum, 1)
            dve.wait_ge(v_sum, 1)
            dve.tensor_scalar(mean[:, 0:TT], mean[:, 8:8 + TT], 1.0 / (GROUPS * P), EPS, ALU.mult, ALU.add)\
                .then_inc(vmean_ready, 1)
            dve.wait_ge(rv_ready, 1)

            def wr_scale(g, par, slot):
                dve.wait_ge(ws_masked, g + 1)
                if not (isinstance(g, int) and g < 2):
                    dve.wait_ge(wr_lo, g - 1)
                dve.tensor_tensor(sg_w[:, par, :].rearrange("p (c t) -> p c t", c=TT),
                                  ring_w[:, slot, :].unsqueeze(1).broadcast_to([P, TT, P]),
                                  r_v[:].unsqueeze(2).broadcast_to([P, TT, P]), ALU.mult)\
                    .then_inc(wr_scaled, 1)

            def wr_part(g, par):
                dve.wait_ge(wr_hi, g + 1)
                dve.tensor_tensor(act_l[:, 16 + par, :], sg_w[:, par, :], act_h[:, 16 + par, :].bitcast(F32),
                                  ALU.subtract).then_inc(wr_lo, 1)

            def mix(g, par, slot, turn):
                dve.wait_ge(mix_full, g + 1)
                dve.wait_ge(b_landed[slot], 16 * (turn + 1))
                if not (isinstance(g, int) and g == 0):
                    dve.wait_ge(gated_lo, g)
                dve.scalar_tensor_tensor(out=sg_s.rearrange("p (c t) -> p c t", c=TT),
                                         in0=ps[:, 4 + par, :].rearrange("p (c t) -> p c t", c=TT),
                                         scalar=colp[:, bass.ds(PC_VG + g, 1)],
                                         in1=ring_b[:, slot, :].unsqueeze(1).broadcast_to([P, TT, P]),
                                         op0=ALU.mult, op1=ALU.add).then_inc(out_free, 1)
                dve.wait_ge(out_free, A_S + g + 1)
                dve.wait_ge(u_gelu, g + 1)
                dve.tensor_tensor(sg_s, sg_s, sg_u[:, par, :], ALU.mult).then_inc(gated, 1)

            def gate_lo(g):
                dve.wait_ge(gated_hi, g + 1)
                dve.tensor_tensor(act_l[:, g, :], sg_s, act_h[:, g, :].bitcast(F32), ALU.subtract)\
                    .then_inc(gated_lo, 1)

            wr_scale(0, 0, 0)
            wr_part(0, 0)

            def u_block(i, first, last):
                for k in range(4):
                    g = 4 * i + k
                    tick(C_U + g, k)
                    dve.wait_ge(chunk_used, C_U + g + 1)
                    if not (first and k < 2):
                        dve.wait_ge(u_gelu, g - 1)
                    dve.tensor_tensor(sg_a[:, k % 2, :], ps[:, k, :], r_row[:], ALU.mult).then_inc(main_free, 1)
                    if not (last and k == 3):
                        wr_scale(g + 1, (k + 1) % 2, (k + 1) % 4)
                    if not (first and k == 0):
                        mix(g - 1, (k + 1) % 2, (k + 3) % 4, i - 1 if k == 0 else i)
                    if not (last and k == 3):
                        wr_part(g + 1, (k + 1) % 2)
                    if not (first and k == 0):
                        gate_lo(g - 1)

            rolled(dve, GROUPS // 4, u_block)
            mix(GROUPS - 1, 1, 3, 3)
            gate_lo(GROUPS - 1)
            project(1, C_OUT, A_OUT, 2, PC_FFN)
            ffn(0, C_UP0, G_UP0)
            project(2, C_DN0, A_DN0, 3, PC_MIX + KT)

            finish_norm(2, C_KV, None)
            dve.tensor_tensor(r2_col[:], r_col[:], r_col[:], ALU.mult).then_inc(rx_ready, 1)
            dve.tensor_scalar(r8_col[:], r_col[:], HD ** -0.5, None, ALU.mult).then_inc(rx_ready, 1)
            for q in range(1, 4):
                tick(C_KV + q, q)
            for t in range(TT):
                if t < TT - 1:
                    dve.wait_ge(kv_full, t + 1)
                else:
                    dve.wait_ge(chunk_used, C_KV + 4)
                dve.tensor_scalar(kv[:, t, :], ps[:, t, :], r_col[:, t:t + 1], None, ALU.mult)\
                    .then_inc(main_free, 1)
                dve.wait_ge(k_squared, t + 1)
                dve.tensor_reduce(mean[:, 32 + 4 * t:36 + 4 * t],
                                  kv_sq[:, t % 2, :].rearrange("p (g d) -> p g d", g=KV_HEADS), AX_X, ALU.add)\
                    .then_inc(k_ss, 1)
            dve.wait_ge(k_ss, TT)
            dve.tensor_scalar(mean[:, 0:16], mean[:, 32:48], 1.0 / HD, EPS, ALU.mult, ALU.add)\
                .then_inc(k_mean, 1)
            for t in range(TT):
                dve.wait_ge(vv_hi, t + 1)
                dve.tensor_tensor(v_parts(v_l, t), kv[:, t, 256:512].rearrange("p (c x d) -> p c x d", c=2, x=2),
                                  v_parts(v_h, t).bitcast(F32), ALU.subtract).then_inc(vv_lo, 1)
            tick(C_Q, 0)
            dve.wait_ge(rk_ready, 1)
            dve.wait_ge(gains_ready, 2)
            for t in range(TT):
                k_view = kv[:, t, 0:256].rearrange("p (g d) -> p g d", g=KV_HEADS)
                n_view = k_n[:, t, :].rearrange("p (g d) -> p g d", g=KV_HEADS)
                dve.tensor_tensor(k_view, k_view, r_k[:, 4 * t:4 * t + 4].unsqueeze(2)
                                  .broadcast_to([P, KV_HEADS, HD]), ALU.mult).then_inc(k_scaled, 1)
                dve.wait_ge(k_scaled, t + 1)
                dve.tensor_tensor(n_view, k_view, qk_gain[:].unsqueeze(1).broadcast_to([P, KV_HEADS, HD]),
                                  ALU.mult).then_inc(k_normed, 1)

            def q_lo(j):
                dve.wait_ge(q_squared, j + 1)
                dve.tensor_tensor(act_l[:, SLOT_Q + j, :], ps[:, B_Q + j % 2, :],
                                  act_h[:, SLOT_Q + j, :].bitcast(F32), ALU.subtract).then_inc(q_free, 1)

            def q_means(j):
                part = slice(8 * j, 8 * j + 8)
                two = lambda x: x.rearrange("p (t x) -> p t x", t=TT)
                dve.wait_ge(q_summed, j + 1)
                dve.wait_ge(rx_ready, 2)
                dve.tensor_tensor(two(r_q[:, part]), two(ps[:, B_Q + j % 2, 0:8]),
                                  r2_col[:].unsqueeze(2).broadcast_to([P, TT, 2]), ALU.mult).then_inc(q_scaled, 1)
                dve.wait_ge(q_scaled, j + 1)
                dve.tensor_scalar(mean[:, part], r_q[:, part], 1.0 / HD, EPS, ALU.mult, ALU.add)\
                    .then_inc(q_mean, 1)

            def q_factors(j):
                part = slice(8 * j, 8 * j + 8)
                two = lambda x: x.rearrange("p (t x) -> p t x", t=TT)
                dve.wait_ge(q_pow, j + 1)
                dve.tensor_tensor(two(r_q[:, part]), two(r_q[:, part]),
                                  r8_col[:].unsqueeze(2).broadcast_to([P, TT, 2]), ALU.mult).then_inc(rq_ready, 1)

            q_lo(0)
            tick(C_Q + 1, 1)
            q_lo(1)
            q_means(0)
            for c in range(2):
                for x in range(2):
                    part = slice(x * HD, (x + 1) * HD)
                    dve.wait_ge(kt_hi, 2 * c + x + 1)
                    dve.tensor_tensor(act_l[part, SLOT_K + 2 * c + x, :], ps[part, B_O + c, :],
                                      act_h[part, SLOT_K + 2 * c + x, :].bitcast(F32), ALU.subtract)\
                        .then_inc(kt_lo, 1)
            q_factors(0)
            tick(C_Q + 2, 2)
            q_means(1)
            q_factors(1)

            def attend(u):
                late = u - WO_STEP - 1
                if late >= 0 and late % 2 == 1:
                    d = late // 2
                    if d % 2:
                        dve.wait_ge(chunk_used, C_WO + d // 2 + 1)
                    else:
                        dve.wait_ge(wo_half, d // 2 + 1)
                    dve.tensor_tensor(h[:, d, :], ps[:, B_Q + d % 2, :], h[:, d, :], ALU.add)\
                        .then_inc(wo_added, 1)
                if u < UNITS:
                    j, n = unit(u)
                    first_key = P if n == 0 else 0
                    if n == 0:
                        dve.wait_ge(rq_ready, j + 1)
                        dve.wait_ge(bias_landed[j // 4], 16)
                    dve.wait_ge(s_full, u + 1)
                    if u >= S_RING:
                        dve.wait_ge(p_turned, u - S_RING + 1)
                    col = 8 * j + 2 * n
                    for x in range(2):
                        dve.scalar_tensor_tensor(out=at_s[:, u % S_RING, x, first_key:],
                                                 in0=ps[:, B_S + u % 2, x * 256 + first_key:(x + 1) * 256],
                                                 scalar=r_q[:, col + x:col + x + 1],
                                                 in1=at_bias[:, 2 * j + x, first_key:],
                                                 op0=ALU.mult, op1=ALU.add).then_inc(s_biased, 1)
                    dve.wait_ge(s_biased, 2 * u + 2)
                    two = slice(2 * u, 2 * u + 2)
                    dve.tensor_reduce(soft[:, 4, two], at_s[:, u % S_RING, :, first_key:], AX_X, ALU.max)\
                        .then_inc(s_max, 1)
                if 1 <= u < UNITS + 1:
                    w = u - 1
                    last = slice(2 * w, 2 * w + 2)
                    dve.wait_ge(sink_exp, w + 1)
                    dve.tensor_tensor(soft[:, 4, last], soft[:, 2, last], soft[:, 3, last], ALU.add).then_inc(den, 1)
                if u < UNITS:
                    dve.wait_ge(s_max, u + 1)
                    dve.scalar_tensor_tensor(out=soft[:, 0, two], in0=soft[:, 4, two], scalar=-1.0,
                                             in1=negsink[:, 2 * j:2 * j + 2], op0=ALU.mult, op1=ALU.min)\
                        .then_inc(m_ready, 1)
                if 1 <= u < UNITS + 1:
                    dve.wait_ge(den, w + 1)
                    dve.reciprocal(soft[:, 5, last], soft[:, 4, last]).then_inc(rden, 1)
                if u < UNITS:
                    dve.wait_ge(m_ready, u + 1)
                    dve.tensor_tensor(soft[:, 1, two], soft[:, 0, two],
                                      rowp[:, PR_SINK + 2 * j:PR_SINK + 2 * j + 2], ALU.add).then_inc(sink_off, 1)
                if u % 4 != 2 and u // 4 + 2 < KT:
                    [q_lo, q_means, None, q_factors][u % 4](u // 4 + 2)
                w = u - LAG_T
                if 0 <= w < UNITS:
                    first_half = 256 if unit(w)[1] == 0 else 0
                    dve.wait_ge(p_hi, w + 1)
                    dve.tensor_tensor(act_l[:, SLOT_P + w % P_RING, first_half:], ps[:, B_T + w % 2, first_half:],
                                      act_h[:, SLOT_P + w % P_RING, first_half:].bitcast(F32), ALU.subtract)\
                        .then_inc(p_lo, 1)
                w = u - LAG_O
                if w % 4 == 3 and 0 <= w < UNITS:
                    dve.wait_ge(o_hi, w // 4 + 1)
                    dve.tensor_tensor(quad(act_l, w // 4), quad_bank(w // 4), quad(act_h, w // 4).bitcast(F32),
                                      ALU.subtract).then_inc(o_lo, 1)

            for u in range(STEPS + 1):
                attend(u)
            dve.wait_ge(lo_split, C_WO + 4 + AHEAD)
            for j in range(KT // 2):
                tick(C_WO + 4 + j, j)
                dve.wait_ge(wo_added, KT)
                for d in (2 * j, 2 * j + 1):
                    if d % 2 == 0:
                        dve.wait_ge(wo_first, j + 1)
                    else:
                        dve.wait_ge(chunk_used, C_WO + 4 + j + 1)
                    dve.tensor_tensor(h[:, d, :], ps[:, 4 + d % 2, :], h[:, d, :], ALU.add).then_inc(out_free, 1)
                    dve.wait_ge(out_free, A_WO + d + 1)
                    spread_lo(3, d, colp[:, PC_FFN + KT + d:PC_FFN + KT + d + 1], d == 0)
            ffn(1, C_UP1, G_UP1)
            project(4, C_DN1, A_DN1, 3, 0)

        @block.tensor
        def _(pe):
            def mm3(dst, stat_h, stat_l, mov_h, mov_l, start, stop):
                pe.matmul(dst, stat_h, mov_h, start=start, stop=False)
                pe.matmul(dst, stat_h, mov_l, start=False, stop=False)
                return pe.matmul(dst, stat_l, mov_h, start=False, stop=stop)

            def norm_sums(n):
                pe.wait_ge(sq_added, KT * (n + 1))
                for t in range(TT):
                    m = pe.matmul(ps[:, MISC, t:t + 1], sq_sum[:, t * P:(t + 1) * P], ones[:, 0:1],
                                  start=True, stop=True)
                m.then_inc(col_summed, 1)

            def norm_row(row):
                pe.wait_ge(diag_ready, row + 1)
                pe.matmul(ps[:, MISC, :], ones[:], sq, start=True, stop=True).then_inc(row_spread, 1)

            def tile_chunk(c, slot, bank, n, wait_tiles):
                pe.wait_ge(lo_split, c + 1)
                for k in range(KT):
                    if wait_tiles:
                        pe.wait_ge(hn_lo, KT * n + k + 1)
                    b = operand_blocks(k)
                    m = mm3(ps[:, bank, :], w_h[:, slot, b], w_l[:, slot, b], hn_h[:, k, :], hn_l[:, k, :],
                            k == 0, k == KT - 1)
                m.then_inc(chunk_used, 1)

            def token_chunk(c, q, full, wait_bank, wait_tiles, n):
                pe.wait_ge(lo_split, c + 1)
                for t in range(TT):
                    if wait_bank is not None and q == 0:
                        pe.wait_ge(main_free, wait_bank + t)
                    for kk in range(2):
                        k = 2 * q + kk
                        if wait_tiles and t == 0:
                            pe.wait_ge(hn_lo, KT * n + k + 1)
                        rows_ = slice(t * P, (t + 1) * P)
                        cols_ = slice(kk * 512, (kk + 1) * 512)
                        start, stop = k == 0, k == KT - 1
                        pe.matmul(ps[:, t, :], hn_h[:, k, rows_], w_h[:, q, cols_], start=start, stop=False)
                        pe.matmul(ps[:, t, :], hn_h[:, k, rows_], w_l[:, q, cols_], start=False, stop=False)
                        m = pe.matmul(ps[:, t, :], hn_l[:, k, rows_], w_h[:, q, cols_], start=False, stop=stop)
                    if t == TT - 1:
                        m.then_inc(chunk_used, 1)
                    elif q == 3:
                        m.then_inc(full, 1)

            def project(base, a_base, chunks, tiles, slot0, ready, r_base, per_tile):
                per = {3: 4, 2: 2, 1: 4}[chunks]

                def body(i, first, last):
                    for dd in range(per):
                        d = i * per + dd
                        a = a_base + d
                        pe.wait_ge(out_free, a - 1)
                        for part in range(chunks):
                            c = base + (i * per + dd) * chunks + part
                            slot = (dd * chunks + part) % RING
                            pe.wait_ge(lo_split, c + 1)
                            for k in range(8 * part, min(8 * part + 8, tiles)):
                                if first and dd == 0:
                                    pe.wait_ge(ready, r_base + per_tile * (k + 1))
                                b = operand_blocks(k % 8)
                                m = mm3(ps[:, 4 + dd % 2, :], w_h[:, slot, b], w_l[:, slot, b],
                                        act_h[:, slot0 + k, :], act_l[:, slot0 + k, :],
                                        k == 0, k == tiles - 1)
                            m.then_inc(chunk_used, 1)

                rolled(pe, KT // per, body)

            def ffn_up(n, base, g_base):
                def body(i, first, last):
                    for k in range(4):
                        pe.wait_ge(main_free, g_base + 4 * i + k - 3)
                        tile_chunk(base + 4 * i + k, k, k, n, first and k == 0)
                        if first and k == 0:
                            norm_sums(n)
                        if first and k == 1:
                            norm_row((n + 1) // 2)

                rolled(pe, PAIRS // 2, body)

            pe.wait_ge(rel_landed, 16 * 3)
            pe.matmul(ps[0:HEADS, 6, 0:384], rel_sb, onehot_sb, start=True, stop=True).then_inc(lines_summed, 1)
            pe.wait_ge(consts_ready, 3)

            def v_block(j, first, last):
                for q in range(4):
                    token_chunk(C_V + 4 * j + q, q, v_full, None if first else G_V + 4 * j - 3, first, 0)

            def v_first():
                for q in range(4):
                    token_chunk(C_V + q, q, v_full, None, True, 0)
                    if q == 2:
                        norm_sums(0)
                    if q == 3:
                        norm_row(0)

            v_first()
            with pe.Fori(1, 4) as j:
                v_block(j, False, False)

            def spatial(g):
                pe.wait_ge(wr_lo, g + 1)
                if g >= 2:
                    pe.wait_ge(out_free, A_S + g - 1)
                for c in range(TT):
                    t = slice(c * P, (c + 1) * P)
                    m = mm3(ps[:, 4 + g % 2, t], act_h[:, g, t], act_l[:, g, t],
                            act_h[:, 16 + g % 2, t], act_l[:, 16 + g % 2, t], True, True)
                m.then_inc(mix_full, 1)

            for g in range(GROUPS):
                pe.wait_ge(main_free, G_U + g - 3)
                tile_chunk(C_U + g, g % 4, g % 4, 0, False)
                if g == 1:
                    pe.wait_ge(v_lo, 16)
                if g >= 1:
                    spatial(g - 1)
            spatial(GROUPS - 1)
            project(C_OUT, A_OUT, 2, GROUPS, 0, gated_lo, 0, 1)
            ffn_up(1, C_UP0, G_UP0)
            project(C_DN0, A_DN0, 3, PAIRS, 0, prod_lo, 0, 1)

            for q in range(4):
                token_chunk(C_KV + q, q, kv_full, G_KV - 3, True, 2)
                if q == 0:
                    norm_sums(2)

            def q_sums(j):
                pe.wait_ge(q_squared, j + 1)
                pe.wait_ge(q_free, j + 1)
                for t in range(TT):
                    m = pe.matmul(ps[:, B_Q + j % 2, 2 * t:2 * t + 2], q_sq[:, t * P:(t + 1) * P],
                                  halves[:], start=True, stop=True)
                m.then_inc(q_summed, 1)

            def q_quarter(j, q):
                c = C_Q + j
                if q == 0:
                    pe.wait_ge(lo_split, c + 1)
                    if j == 1:
                        pe.wait_ge(mean_ready, 3)
                    elif j >= 2:
                        pe.wait_ge(q_scaled, j - 1)
                for k in (2 * q, 2 * q + 1):
                    b = operand_blocks(k)
                    m = mm3(ps[:, B_Q + j % 2, :], w_h[:, c % RING, b], w_l[:, c % RING, b], hn_h[:, k, :],
                            hn_l[:, k, :], k == 0, k == KT - 1)
                if q == 3:
                    m.then_inc(chunk_used, 1)

            def wo_quarter(w):
                c, d = C_WO + w // 4, w // 2
                if w == 0:
                    pe.wait_ge(o_lo, 4)
                    pe.wait_ge(q_scaled, KT)
                if w % 4 == 0:
                    pe.wait_ge(lo_split, c + 1)
                if w % 2 == 0 and d >= 2:
                    pe.wait_ge(wo_added, d - 1)
                for k in (2 * (w % 2), 2 * (w % 2) + 1):
                    b = operand_blocks(4 * (d % 2) + k)
                    m = mm3(ps[:, B_Q + d % 2, :], w_h[:, c % RING, b], w_l[:, c % RING, b], act_h[:, k, :],
                            act_l[:, k, :], k == 0, k == 3)
                if w % 2 == 1:
                    m.then_inc(chunk_used if d % 2 else wo_half, 1)

            def turn_k(c):
                for t in range(TT):
                    pe.wait_ge(k_normed, t + 1)
                    pe.transpose(ps[:, B_O + c, t * P:(t + 1) * P], k_n[:, t, c * P:(c + 1) * P], ident[:])\
                        .then_inc(k_turned, 1)

            pe.wait_ge(halves_ready, 3)
            for q in range(4):
                q_quarter(0, q)
            for q in range(4):
                q_quarter(1, q)
            q_sums(0)
            pe.wait_ge(out_free, A_DN0 + KT)
            turn_k(0)
            turn_k(1)
            for q in range(4):
                q_quarter(2, q)
            q_sums(1)

            def attend(u):
                if u % 4 == 1 and u // 4 + 2 < KT:
                    q_sums(u // 4 + 2)
                w = u - LAG_T
                if 0 <= w < UNITS:
                    pe.wait_ge(p_scaled, 2 * w + 2)
                    if w >= 2:
                        pe.wait_ge(p_lo, w - 1)
                    for half in range(1 if unit(w)[1] == 0 else 0, 2):
                        for x in range(2):
                            m = pe.transpose(ps[:, B_T + w % 2, (2 * half + x) * P:(2 * half + x + 1) * P],
                                             at_s[:, w % S_RING, x, half * P:(half + 1) * P], ident[:])
                    m.then_inc(p_turned, 1)
                if u < UNITS:
                    j, n = unit(u)
                    if u == 0:
                        pe.wait_ge(kt_lo, 4)
                        pe.wait_ge(padded, 4)
                    if n == 0:
                        pe.wait_ge(q_free, j + 1)
                    if u >= 2:
                        pe.wait_ge(s_biased, 2 * u - 2)
                    first_key = P if n == 0 else 0
                    keys = slice((n - 1) * P + first_key, (n + 1) * P)
                    q = slice(n * P, (n + 1) * P)
                    for x in range(2):
                        k_slot = SLOT_K + 2 * (j // 4) + x
                        m = mm3(ps[:, B_S + u % 2, x * 256 + first_key:(x + 1) * 256], act_h[:, j, q], act_l[:, j, q],
                                act_h[:, k_slot, keys], act_l[:, k_slot, keys], True, True)
                    m.then_inc(s_full, 1)
                w = u - LAG_PV
                if w % 2 == 1 and 0 <= w < UNITS:
                    j, n = unit(w)
                    if w % 4 == 1 and w >= 8:
                        pe.wait_ge(o_lo, w // 4 - 1)
                    pe.wait_ge(p_lo, w + 1)
                    if w == 1:
                        pe.wait_ge(vv_lo, TT)
                    slot = SLOT_P + (w - 1) % P_RING
                    terms = [(half, x) for half in ([1] if n == 0 else [0, 1]) for x in range(2)]
                    for half, x in terms:
                        v = (n - 1 + half) * 384 + j // 4 * 192 + x * HD
                        pt = slice(half * 256 + x * P, half * 256 + (x + 1) * P)
                        m = mm3(ps[:, B_O + w // 4 % 2, n % 2 * 256:n % 2 * 256 + 256], v_h[:, v:v + P],
                                v_l[:, v:v + P], act_h[:, slot:slot + 2, pt], act_l[:, slot:slot + 2, pt],
                                (half, x) == terms[0], (half, x) == terms[-1])
                    m.then_inc(o_full, 1)
                if u < 4 * (KT - Q_EARLY):
                    q_quarter(u // 4 + Q_EARLY, u % 4)
                elif u >= WO_STEP:
                    wo_quarter(u - WO_STEP)

            for u in range(STEPS):
                attend(u)
            for j in range(KT // 2):
                c = C_WO + 4 + j
                pe.wait_ge(lo_split, c + 1)
                for d in (2 * j, 2 * j + 1):
                    if d >= 2:
                        pe.wait_ge(out_free, A_WO + d - 1)
                    for k in range(4):
                        if d == 0:
                            pe.wait_ge(o_lo, KT)
                        b = operand_blocks(4 * (d % 2) + k)
                        m = mm3(ps[:, 4 + d % 2, :], w_h[:, j, b], w_l[:, j, b], act_h[:, 4 + k, :],
                                act_l[:, 4 + k, :], k == 0, k == 3)
                    m.then_inc(wo_first if d % 2 == 0 else chunk_used, 1)
            ffn_up(3, C_UP1, G_UP1)
            project(C_DN1, A_DN1, 3, PAIRS, 0, prod_lo, PAIRS, 1)


def bucket_of_distance():
    n = np.arange(MAX_DIST)
    exact = BUCKETS // 2
    large = exact + (np.log(np.maximum(n, 1).astype(np.float32) / exact)
                     / math.log(MAX_DIST / exact) * (BUCKETS - exact)).astype(np.int32)
    return np.where(n < exact, n, np.minimum(large, BUCKETS - 1))


def constants():
    onehot = np.zeros((BUCKETS, 384), np.float32)
    masked = np.full((HEADS, 384), MASKED, np.float32)
    for dist, b in enumerate(bucket_of_distance()):
        onehot[b, 255 - dist] = 1.0
        masked[:, 255 - dist] = 0.0
    return onehot, masked


def kernel(**inputs):
    import concourse.bacc as bacc
    from concourse.bass_utils import run_bass_kernel_spmd

    a = {k: np.asarray(v) for k, v in inputs.items()}

    def by_tile(w):
        k, n = w.shape
        blocks = w.reshape(k // P, P, n // P, P).transpose(2, 1, 0, 3)
        parts = []
        for tile in blocks:
            for lo in range(0, k // P, 8):
                part = tile[:, lo:lo + 8].reshape(P, -1)
                parts.append(np.pad(part, ((0, 0), (0, CHUNK - part.shape[1]))))
        return np.stack(parts)

    def by_token(w):
        n = w.shape[1]
        return w.reshape(4, 2, P, n // 512, 512).transpose(3, 0, 2, 1, 4).reshape(-1, P, CHUNK)

    def by_halves(w):
        return w.reshape(2, 4, P, 4, 2, P).transpose(0, 3, 2, 4, 1, 5).reshape(-1, P, CHUNK)

    def pairs(w, axis):
        w = np.moveaxis(w, axis, -1)
        w = w.reshape(w.shape[:-1] + (2, PAIRS, P))
        w = np.swapaxes(w, -3, -2)
        return np.moveaxis(w.reshape(w.shape[:-3] + (2 * PAIRS * P,)), -1, axis)

    heads = np.arange(HEADS).reshape(2, 2, 4).transpose(0, 2, 1).reshape(-1)
    w_in = a["sgu_w_in"][0]
    w_qkv = a["attn_w_qkv"][0]
    w_q = w_qkv[:, :D_MODEL].reshape(D_MODEL, HEADS, HD)[:, heads].reshape(D_MODEL, D_MODEL)
    w_o = a["attn_w_o"][0].reshape(HEADS, HD, D_MODEL)[heads].reshape(D_MODEL, D_MODEL)
    stream = np.concatenate([
        by_token(w_in[:, 2 * D_MODEL:]), by_tile(w_in[:, :2 * D_MODEL]), by_tile(a["sgu_w_out"][0]),
        by_tile(pairs(a["ffn_w_up"][0], 1)), by_tile(a["ffn_w_down"][0]),
        by_token(w_qkv[:, D_MODEL:]), by_tile(w_q), by_halves(w_o),
        by_tile(pairs(a["ffn_w_up"][1], 1)), by_tile(a["ffn_w_down"][1])])
    down = lambda v: v.reshape(-1, P).T
    conv = [np.stack([*pairs(a["ffn_conv_w"][i], 1), pairs(a["ffn_conv_b"][i], 0)], -1)
            .reshape(2 * PAIRS, P, 4).transpose(1, 0, 2).reshape(P, -1) for i in range(2)]
    cols = np.concatenate([down(a["mix_norm"]), down(a["ffn_norm"]), down(a["sgu_v_gain"][0]), *conv], 1)
    rows = np.concatenate([a["attn_q_gain"][0], a["attn_k_gain"][0], a["attn_sinks"][0][heads]])
    onehot, masked = constants()
    arrays = {
        "x_t": a["x"][0].T.reshape(KT, P, SEQ),
        "stream": stream,
        "cols": cols,
        "rows": rows,
        "ws_t": a["sgu_w_s"][0].transpose(0, 2, 1),
        "b_s": a["sgu_b_s"][0],
        "rel": a["rel_bias"][:, heads],
        "onehot": onehot,
        "masked": masked,
    }
    arrays = {k: np.ascontiguousarray(v) for k, v in arrays.items()}
    nc = bacc.Bacc("TRN2", target_bir_lowering=False, num_devices=1)
    args = [nc.dram_tensor(k, v.shape, F32, kind="ExternalInput").ap() for k, v in arrays.items()]
    args.append(nc.dram_tensor("out_t", (KT, P, SEQ), F32, kind="ExternalOutput").ap())
    build(nc, *args)
    r = run_bass_kernel_spmd(nc, [arrays], core_ids=[0])
    return np.ascontiguousarray(r.results[0]["out_t"].reshape(D_MODEL, SEQ).T)[None]
```

```python
import math
from contextlib import ExitStack

import numpy as np

import concourse.bass as bass
from concourse import mybir

F32 = mybir.dt.float32
F32R = mybir.dt.float32r
ALU = mybir.AluOpType
ACT = mybir.ActivationFunctionType
AX_X = mybir.AxisListType.X

P = 128
D_MODEL = 1024
SEQ = 512
KT = D_MODEL // P
TT = SEQ // P
GROUPS = 16
HEADS = 16
KV_HEADS = 4
HD = 64
D_FF = 2816
PAIRS = D_FF // P
BUCKETS = 32
MAX_DIST = 128
EPS = 1e-6
MASKED = -1e30

CHUNK = 1024
C_V = 0
C_U = C_V + 16
C_OUT = C_U + 16
C_UP0 = C_OUT + 2 * KT
C_DN0 = C_UP0 + 2 * PAIRS
C_KV = C_DN0 + 3 * KT
C_Q = C_KV + 4
C_WO = C_Q + KT
C_UP1 = C_WO + KT
C_DN1 = C_UP1 + 2 * PAIRS
CHUNKS = C_DN1 + 3 * KT
RING = 4
RAW = 2
AHEAD = 3

G_V, G_U, G_UP0, G_KV, G_UP1 = 0, 16, 32, 76, 80
A_S, A_OUT, A_DN0, A_WO, A_DN1 = 0, 16, 24, 32, 40
MISC = 7
B_S, B_T, B_O, B_Q = 0, 2, 4, 6

PC_MIX, PC_FFN, PC_VG, PC_CONV = 0, 2 * KT, 4 * KT, 4 * KT + GROUPS
PC_ALL = PC_CONV + 2 * 2 * PAIRS * 4
PR_QG, PR_KG, PR_SINK, PR_ALL = 0, HD, 2 * HD, 2 * HD + HEADS

SLOT_W = GROUPS
SLOT_Q, SLOT_K, SLOT_V, SLOT_P = 0, 8, 12, 15
P_RING = 4
S_RING = 3
UNITS = KT * TT
Q_EARLY = 3
WO_STEP = 22
STEPS = WO_STEP + 16
WARM_UP = 18
LAG_T, LAG_PV, LAG_O = 3, 5, 5


def rolled(eng, n, body):
    body(0, True, n == 1)
    if n > 3:
        with eng.Fori(1, n - 1) as i:
            body(i, False, False)
    else:
        for i in range(1, n - 1):
            body(i, False, False)
    if n > 1:
        body(n - 1, False, True)


def build(nc, x_t, stream, cols, rows, ws_t, b_s, rel, onehot, masked, out_t):
    ctx = ExitStack()
    with ctx:
        def sb(name, shape, dt=F32):
            return ctx.enter_context(nc.sbuf_tensor(name, shape, dt))

        def sem(name):
            return ctx.enter_context(nc.semaphore(name))

        ps = ctx.enter_context(nc.psum_tensor("ps", [P, 8, 512], F32))
        h = sb("h", [P, KT, SEQ])
        hn_h = sb("hn_h", [P, KT, SEQ], F32R)
        hn_l = sb("hn_l", [P, KT, SEQ], F32R)
        act_h = sb("act_h", [P, PAIRS, SEQ], F32R)
        act_l = sb("act_l", [P, PAIRS, SEQ], F32R)
        raw = sb("raw", [P, RAW, CHUNK])
        w_h = sb("w_h", [P, RING, CHUNK], F32R)
        w_l = sb("w_l", [P, RING, CHUNK], F32R)
        work = sb("work", [P, 5632])
        r_row = sb("r_row", [P, SEQ])
        ident = sb("ident", [P, P])
        ones = sb("ones", [P, P])
        ones_r = sb("ones_r", [P, 1])
        halves = sb("halves", [P, 2])
        colp = sb("colp", [P, PC_ALL])
        rowp = sb("rowp", [P, PR_ALL])
        negsink = sb("negsink", [P, HEADS])
        qk_gain = sb("qk_gain", [P, HD])
        half_neg = sb("half_neg", [P, TT * KV_HEADS])
        mean = sb("mean", [P, 64])
        r_col = sb("r_col", [P, TT])
        r_v = sb("r_v", [P, TT])
        r2_col = sb("r2_col", [P, TT])
        r8_col = sb("r8_col", [P, TT])
        v_sq = sb("v_sq", [P, TT, 4])
        r_k = sb("r_k", [P, TT * KV_HEADS])
        r_q = sb("r_q", [P, 64])
        soft = sb("soft", [P, 6, 2 * UNITS])
        q_plain = sb("q_plain", [P, SEQ])

        sq = work[:, 4608:5120]
        sq_sum = work[:, 5120:5632]
        sq_start = [sq, work[:, 3072:3584]]
        diag = sq.rearrange("p (t q) -> p t q", t=TT)
        ff_a = work[:, 0:2 * 514].rearrange("p (r n) -> p r n", r=2)
        ff_c = work[:, 1028:1028 + 2048].rearrange("p (r n) -> p r n", r=4)
        ff_p = work[:, 3076:3076 + 1024].rearrange("p (r n) -> p r n", r=2)
        sg_a = work[:, 0:1024].rearrange("p (r n) -> p r n", r=2)
        sg_u = work[:, 1024:2048].rearrange("p (r n) -> p r n", r=2)
        sg_w = work[:, 2048:3072].rearrange("p (r n) -> p r n", r=2)
        sg_s = [sq, work[:, 3072:3584]]
        ring_w = work[:, 3584:4096].rearrange("p (r n) -> p r n", r=4)
        ring_b = work[:, 4096:4608].rearrange("p (r n) -> p r n", r=4)
        at_bias = work[:, 0:4096].rearrange("p (g n) -> p g n", g=HEADS)
        at_s = work[:, 4096:5632].rearrange("p (r x n) -> p r x n", r=S_RING, x=2)
        kv = work[:, 0:2048].rearrange("p (t n) -> p t n", t=TT)
        kv_sq = work[:, 2048:2560].rearrange("p (r n) -> p r n", r=2)
        q_sq = r_row
        line_sb = soft[0:HEADS, :, :].rearrange("p a b -> p (a b)")
        k_n = work[:, 3584:4608].rearrange("p (t n) -> p t n", t=TT)
        rel_sb = work[0:BUCKETS, 0:HEADS]
        onehot_sb = work[0:BUCKETS, 512:896]
        masked_sb = work[0:HEADS, 1024:1408]
        v_h = act_h[:, SLOT_V:SLOT_V + 3, :].rearrange("p s n -> p (s n)")
        v_l = act_l[:, SLOT_V:SLOT_V + 3, :].rearrange("p s n -> p (s n)")

        def v_parts(v, t):
            return v[:, t * 384:(t + 1) * 384].rearrange("p (c z d) -> p c z d", c=2, z=3)[:, :, 0:3:2, :]

        def v_zeros(v):
            return v.rearrange("p (m z d) -> p m z d", m=2 * TT, z=3)[:, :, 1, :]

        lines = nc.dram_tensor("rel_lines", (HEADS, P, 384), F32, kind="Internal").ap()

        params_landed = sem("params_landed")
        rows_landed = sem("rows_landed")
        rel_landed = sem("rel_landed")
        x_landed = [sem(f"x_landed{d}") for d in range(KT)]
        raw_landed = [sem(f"raw_landed{s}") for s in range(RAW)]
        ws_landed = [sem(f"ws_landed{s}") for s in range(4)]
        b_landed = [sem(f"b_landed{s}") for s in range(4)]
        lines_stored = sem("lines_stored")
        bias_landed = [sem(f"bias_landed{c}") for c in range(2)]
        out_stored = sem("out_stored")
        hi_split = sem("hi_split")
        lo_split = sem("lo_split")
        lo_half = sem("lo_half")
        chunk_used = sem("chunk_used")
        main_free = sem("main_free")
        out_free = sem("out_free")
        consts_zeroed = sem("consts_zeroed")
        consts_ready = sem("consts_ready")
        halves_ready = sem("halves_ready")
        table_loaded = sem("table_loaded")
        warmed = sem("warmed")
        gains_ready = sem("gains_ready")
        lines_summed = sem("lines_summed")
        lines_ready = sem("lines_ready")
        pads_zeroed = sem("pads_zeroed")
        hn_hi = sem("hn_hi")
        hn_lo = sem("hn_lo")
        squared = sem("squared")
        sq_added = sem("sq_added")
        col_summed = sem("col_summed")
        mean_ready = sem("mean_ready")
        r_ready = sem("r_ready")
        diag_ready = sem("diag_ready")
        row_spread = sem("row_spread")
        row_ready = sem("row_ready")
        v_full = sem("v_full")
        v_gelu = sem("v_gelu")
        v_squared = sem("v_squared")
        v_hi = sem("v_hi")
        v_lo = sem("v_lo")
        v_sum = sem("v_sum")
        vmean_ready = sem("vmean_ready")
        rv_ready = sem("rv_ready")
        ws_masked = sem("ws_masked")
        wr_scaled = sem("wr_scaled")
        wr_hi = sem("wr_hi")
        wr_lo = sem("wr_lo")
        u_gelu = sem("u_gelu")
        mix_full = sem("mix_full")
        mixed = sem("mixed")
        gated = sem("gated")
        gated_hi = sem("gated_hi")
        gated_lo = sem("gated_lo")
        conv_0 = sem("conv_0")
        conv_1 = sem("conv_1")
        conv_2 = sem("conv_2")
        silu_done = sem("silu_done")
        prod = sem("prod")
        prod_hi = sem("prod_hi")
        prod_lo = sem("prod_lo")
        kv_full = sem("kv_full")
        padded = sem("padded")
        vv_hi = sem("vv_hi")
        vv_lo = sem("vv_lo")
        k_squared = sem("k_squared")
        k_ss = sem("k_ss")
        k_mean = sem("k_mean")
        rk_ready = sem("rk_ready")
        k_scaled = sem("k_scaled")
        k_normed = sem("k_normed")
        k_turned = sem("k_turned")
        kt_hi = sem("kt_hi")
        kt_lo = sem("kt_lo")
        q_hi = sem("q_hi")
        q_squared = sem("q_squared")
        q_split = sem("q_split")
        q_copied = sem("q_copied")
        wo_half = sem("wo_half")
        wo_added = sem("wo_added")
        wo_even_full = sem("wo_even_full")
        q_summed = sem("q_summed")
        rx_ready = sem("rx_ready")
        q_scaled = sem("q_scaled")
        q_mean = sem("q_mean")
        q_pow = sem("q_pow")
        rq_ready = sem("rq_ready")
        s_full = sem("s_full")
        s_biased = sem("s_biased")
        s_max = sem("s_max")
        m_ready = sem("m_ready")
        sink_off = sem("sink_off")
        p_exp = sem("p_exp")
        sink_exp = sem("sink_exp")
        den = sem("den")
        rden = sem("rden")
        p_scaled = sem("p_scaled")
        p_turned = sem("p_turned")
        p_hi = sem("p_hi")
        p_lo = sem("p_lo")
        o_full = sem("o_full")
        o_hi = sem("o_hi")
        o_lo = sem("o_lo")

        block = ctx.enter_context(nc.Block())

        def operand_blocks(kb):
            return slice(kb * P, (kb + 1) * P)

        def filler_chunk(u):
            if 0 <= u < 4 * (KT - Q_EARLY) and u % 4 == 0:
                return C_Q + Q_EARLY + u // 4
            if WO_STEP <= u < STEPS and (u - WO_STEP) % 4 == 0:
                return C_WO + (u - WO_STEP) // 4
            return None

        def unit(u):
            return 2 * (u // 8) + u % 2, 2 * (u // 4 % 2) + u % 4 // 2

        def quad(x, q):
            n = q % 2 * 2 * P
            return x[:, 2 * (q // 2):2 * (q // 2) + 2, n:n + 2 * P].rearrange("p i (n q) -> p i n q", n=2)

        def quad_bank(q):
            return ps[:, B_O + q % 2, :].rearrange("p (n i q) -> p i n q", n=2, i=2)

        def settle(eng):
            eng.wait_ge(params_landed, 16)

        @block.sync
        def _(sp):
            def load(c, slot, again):
                if again:
                    sp.wait_ge(lo_split, c - RAW + 1)
                sp.dma_start(raw[:, slot, :], stream[c]).then_inc(raw_landed[slot], 16)

            sp.dma_start(colp[:], cols).then_inc(params_landed, 16)
            for d in range(KT):
                if d % 3 == 0 and d // 3 < RAW:
                    load(d // 3, d // 3, False)
                sp.dma_start(h[:, d, :], x_t[d]).then_inc(x_landed[d], 16)
            sp.dma_start(rowp[:], rows.partition_broadcast(P)).then_inc(rows_landed, 16)
            with sp.Fori(1, CHUNKS // RAW) as i:
                for k in range(RAW):
                    load(RAW * i + k, k, True)
            for d in range(KT):
                sp.wait_ge(out_free, A_DN1 + d + 1)
                sp.dma_start(out_t[d], h[:, d, :]).then_inc(out_stored, 16)
            sp.wait_ge(out_stored, 16 * KT)

        @block.gpsimd
        def _(pool):
            pool.memset(ones[:], 1.0).then_inc(consts_ready, 1)
            pool.memset(ident[:], 0.0).then_inc(consts_zeroed, 1)
            pool.wait_ge(consts_zeroed, 1)
            pool.affine_select(out=ident[:], in_=ident[:], compare_op=ALU.not_equal, fill=1.0, base=0,
                               pattern=[[-1, P]], channel_multiplier=1).then_inc(consts_ready, 1)
            pool.memset(half_neg[:], -0.5).then_inc(consts_ready, 1)
            pool.wait_ge(consts_ready, 3)

            pool.dma_start(rel_sb, rel).then_inc(rel_landed, 16)
            pool.dma_start(onehot_sb, onehot).then_inc(rel_landed, 16)
            pool.dma_start(masked_sb, masked).then_inc(rel_landed, 16)

            def root(n_sem, n, dst, width, done):
                pool.wait_ge(n_sem, n)
                pool.tensor_tensor(dst, mean[:, 0:width], half_neg[:, 0:width], ALU.pow)\
                    .then_inc(done, 1)

            root(mean_ready, 1, r_col[:], TT, r_ready)

            def fetch(g, s):
                if g >= 4:
                    pool.wait_ge(wr_scaled, g - 3)
                    pool.wait_ge(out_free, A_S + g - 3)
                pool.dma_start(ring_w[:, s, :], ws_t[g]).then_inc(ws_landed[s], 16)
                pool.dma_start(ring_b[:, s, :], b_s[g].partition_broadcast(P)).then_inc(b_landed[s], 16)

            def mask(g, s, turn):
                pool.wait_ge(ws_landed[s], 16 * (turn + 1))
                pool.affine_select(out=ring_w[:, s, :], in_=ring_w[:, s, :], compare_op=ALU.is_ge, fill=0.0,
                                   base=0, pattern=[[1, P]], channel_multiplier=-1).then_inc(ws_masked, 1)

            for g in range(4):
                fetch(g, g)
            for g in range(4):
                mask(g, g, 0)
            root(vmean_ready, 1, r_v[:], TT, rv_ready)
            for g in range(GROUPS):
                pool.wait_ge(ws_masked, g + 1)
                if g == 0:
                    pool.wait_ge(rv_ready, 1)
                elif g >= 2:
                    pool.wait_ge(wr_lo, g - 1)
                pool.tensor_tensor(sg_w[:, g % 2, :].rearrange("p (c t) -> p c t", c=TT),
                                   ring_w[:, g % 4, :].unsqueeze(1).broadcast_to([P, TT, P]),
                                   r_v[:].unsqueeze(2).broadcast_to([P, TT, P]), ALU.mult).then_inc(wr_scaled, 1)
                if 4 <= g + 2 < GROUPS:
                    fetch(g + 2, (g + 2) % 4)
                if 4 <= g + 1 < GROUPS:
                    mask(g + 1, (g + 1) % 4, (g + 1) // 4)
                if g == 1:
                    pool.wait_ge(lines_ready, 1)
                    pool.dma_start(lines, line_sb.unsqueeze(1).broadcast_to([HEADS, P, 384]))\
                        .then_inc(lines_stored, 16)
            root(mean_ready, 2, r_col[:], TT, r_ready)
            root(mean_ready, 3, r_col[:], TT, r_ready)
            pool.wait_ge(chunk_used, C_KV)
            pool.wait_ge(r_ready, 3)
            pads = [act[rows_, SLOT_K + x:SLOT_K + 4:2, :] for act in (act_h, act_l)
                    for x, rows_ in ((0, slice(HD, P)), (1, slice(0, HD)))]
            for i, part in enumerate([*pads, v_zeros(v_h), v_zeros(v_l)]):
                pool.memset(part.bitcast(F32), 0.0).then_inc(padded, 1)
                pool.wait_ge(padded, i + 1)
            root(k_mean, 1, r_k[:], TT * KV_HEADS, rk_ready)

            def q_root(j):
                part = slice(8 * j, 8 * j + 8)
                pool.wait_ge(q_mean, j + 1)
                pool.tensor_tensor(r_q[:, part], mean[:, part], half_neg[:, 0:8], ALU.pow).then_inc(q_pow, 1)

            q_root(0)
            q_root(1)
            pool.wait_ge(lo_split, C_Q + Q_EARLY + AHEAD)
            for u in range(STEPS + 1):
                if u % 4 == 1 and u // 4 + 2 < KT:
                    jq = u // 4 + 2
                    pool.wait_ge(q_hi, jq + 1)
                    pool.wait_ge(q_copied, jq - 1)
                    pool.tensor_tensor(act_l[:, SLOT_Q + jq, :], q_plain[:],
                                       act_h[:, SLOT_Q + jq, :].bitcast(F32), ALU.subtract).then_inc(q_split, 1)
                if 1 <= u < UNITS + 1:
                    w = u - 1
                    first_key = P if unit(w)[1] == 0 else 0
                    pool.wait_ge(rden, w + 1)
                    for x in range(2):
                        part = at_s[:, w % S_RING, x, first_key:]
                        pool.tensor_scalar(part, part, soft[:, 5, 2 * w + x:2 * w + x + 1], 1.0, ALU.mult,
                                           ALU.mult).then_inc(p_scaled, 1)
                if u % 4 == 3 and u // 4 + 2 < KT:
                    q_root(u // 4 + 2)
                for half in range(2):
                    back = 1 + half if u < WO_STEP else 2 + half
                    if filler_chunk(u - back) is not None:
                        c = filler_chunk(u - back) + AHEAD
                        pool.wait_ge(hi_split, c + 1)
                        if half:
                            pool.wait_ge(lo_half, c - AHEAD - C_Q - Q_EARLY + 1)
                        part = slice(half * CHUNK // 2, (half + 1) * CHUNK // 2)
                        pool.tensor_tensor(w_l[:, c % RING, part], raw[:, c % RAW, part],
                                           w_h[:, c % RING, part].bitcast(F32), ALU.subtract)\
                            .then_inc(lo_split if half else lo_half, 1)
            for d in range(KT):
                pool.wait_ge(squared, KT * 3 + d + 1)
                if d == 0:
                    pool.tensor_copy(sq_sum, sq).then_inc(sq_added, 1)
                else:
                    pool.wait_ge(sq_added, KT * 3 + d)
                    pool.tensor_tensor(sq_sum, sq_sum, sq, ALU.add).then_inc(sq_added, 1)
            root(mean_ready, 4, r_col[:], TT, r_ready)

        @block.scalar
        def _(act):
            def tick(c, slot):
                if isinstance(c, int) and c + AHEAD >= CHUNKS:
                    return
                split(c + AHEAD, (slot + AHEAD) % RING, True)

            def split(c, slot, again):
                act.wait_ge(raw_landed[slot % RAW], 16 * (c // RAW + 1) if isinstance(c, int)
                            else (c - slot % RAW) * (16 // RAW) + 16)
                if again and not (isinstance(c, int) and c < RING):
                    act.wait_ge(chunk_used, c - RING + 1)
                act.activation(w_h[:, slot, :], raw[:, slot % RAW, :], ACT.Copy).then_inc(hi_split, 1)

            def spread_hi(n, d, gain, ready, count, first):
                if not first:
                    act.wait_ge(sq_added, KT * n + d)
                act.wait_ge(ready, count)
                settle(act)
                act.activation(hn_h[:, d, :], h[:, d, :], ACT.Copy, scale=gain).then_inc(hn_hi, 1)
                act.activation(sq, h[:, d, :], ACT.Square).then_inc(squared, 1)

            def project(n, base, a_base, chunks, gain_col):
                per = {3: 4, 2: 2, 1: 4}[chunks]

                def body(i, first, last):
                    for dd in range(per):
                        d = i * per + dd
                        for k in range(chunks):
                            tick(base + (i * per + dd) * chunks + k, (dd * chunks + k) % RING)
                        if n < 4:
                            spread_hi(n, d, colp[:, gain_col + d:gain_col + d + 1] if isinstance(d, int)
                                      else colp[:, bass.ds(gain_col + d, 1)], out_free, a_base + d + 1,
                                      first and dd == 0)

                rolled(act, KT // per, body)

            def ffn(layer, base, g_base):
                def body(i, first, last):
                    for k in range(4):
                        tile = 4 * i + k
                        g = g_base + tile
                        n = 44 * layer + tile
                        pair = PAIRS * layer + 2 * i + k // 2
                        if k % 2 == 0 and not (first and k == 0):
                            pp = 2 * i + k // 2 - 1
                            act.wait_ge(prod, pair)
                            settle(act)
                            act.activation(act_h[:, pp, :], ff_p[:, (k // 2 + 1) % 2, :], ACT.Copy)\
                                .then_inc(prod_hi, 1)
                        if not (first and k < 2):
                            tick(base + tile, k)
                        if k % 2 == 1:
                            act.wait_ge(conv_2, n)
                            act.activation(ff_c[:, k - 1, :], ff_c[:, k - 1, :], ACT.Silu)\
                                .then_inc(silu_done, 1)
                        act.wait_ge(main_free, g + 1)
                        if not (first and layer == 0):
                            act.wait_ge(prod, pair - 1)
                        settle(act)
                        pc = PC_CONV + 4 * (44 * layer + tile)
                        act.activation(ff_c[:, k, :], ff_a[:, k % 2, 2:514], ACT.Identity,
                                       bias=colp[:, bass.ds(pc + 3, 1)], scale=colp[:, bass.ds(pc + 2, 1)])\
                            .then_inc(conv_0, 1)

                tick(base, 0)
                tick(base + 1, 1)
                rolled(act, PAIRS // 2, body)
                act.wait_ge(prod, PAIRS * (layer + 1))
                act.activation(act_h[:, PAIRS - 1, :], ff_p[:, 1, :], ACT.Copy).then_inc(prod_hi, 1)

            act.wait_ge(consts_ready, 1)
            act.activation(ones_r[:], ones[:, 0:1], ACT.Copy).then_inc(table_loaded, 1)
            act.wait_ge(params_landed, 16)
            for d in range(KT):
                if d % 3 == 0 and d // 3 < RAW:
                    split(d // 3, d // 3, False)
                act.wait_ge(x_landed[d], 16)
                act.activation(hn_h[:, d, :], h[:, d, :], ACT.Copy, scale=colp[:, PC_MIX + d:PC_MIX + d + 1])\
                    .then_inc(hn_hi, 1)
            for d in range(KT):
                if d == 2:
                    split(2, 2, False)
                if d >= 2:
                    act.wait_ge(sq_added, d - 1)
                act.activation(sq_start[d % 2], h[:, d, :], ACT.Square).then_inc(squared, 1)

            def v_block(j, first, last):
                for q in range(3 if first else 4):
                    tick(C_V + 4 * j + q, q)
                for t in range(TT):
                    if first and t == 2:
                        tick(C_V + 4 * j + 3, 3)
                    u = 4 * j + t
                    act.wait_ge(main_free, G_V + u + 1)
                    if not (first and t < 2):
                        act.wait_ge(v_lo, u - 1)
                    act.activation(sg_u[:, t % 2, :], sg_a[:, t % 2, :], ACT.Gelu).then_inc(v_gelu, 1)
                    act.wait_ge(v_gelu, u + 1)
                    settle(act)
                    act.activation(sg_w[:, 0, :], sg_u[:, t % 2, :], ACT.Square,
                                   accum_out=v_sq[:, t, bass.ds(j, 1)]).then_inc(v_squared, 1)
                    act.activation(act_h[:, bass.ds(4 * j, 4), t * P:(t + 1) * P],
                                   sg_u[:, t % 2, :].rearrange("p (g d) -> p g d", g=4), ACT.Copy)\
                        .then_inc(v_hi, 1)
                    act.wait_ge(v_squared, u + 1)

            rolled(act, 4, v_block)

            def wr_part(g, par):
                act.wait_ge(wr_scaled, g + 1)
                if not (isinstance(g, int) and g < 2):
                    act.wait_ge(mix_full, g - 1)
                act.activation(act_h[:, SLOT_W + par, :], sg_w[:, par, :], ACT.Copy).then_inc(wr_hi, 1)

            def gate_hi(g, par):
                act.wait_ge(gated, g + 1)
                settle(act)
                act.activation(act_h[:, g, :], sg_s[par], ACT.Copy).then_inc(gated_hi, 1)

            wr_part(0, 0)

            def u_block(i, first, last):
                for k in range(4):
                    g = 4 * i + k
                    if not (last and k == 3):
                        wr_part(g + 1, (k + 1) % 2)
                    act.wait_ge(main_free, G_U + g + 1)
                    if not (first and k < 2):
                        act.wait_ge(gated, g - 1)
                    act.activation(sg_u[:, k % 2, :], sg_a[:, k % 2, :], ACT.Gelu).then_inc(u_gelu, 1)
                    tick(C_U + g, k)
                    if not (first and k == 0):
                        gate_hi(g - 1, (k + 1) % 2)

            rolled(act, GROUPS // 4, u_block)
            gate_hi(GROUPS - 1, 1)
            project(1, C_OUT, A_OUT, 2, PC_FFN)
            ffn(0, C_UP0, G_UP0)
            project(2, C_DN0, A_DN0, 3, PC_MIX + KT)

            for q in range(4):
                tick(C_KV + q, q)
            act.wait_ge(padded, 6)
            for t in range(TT):
                act.wait_ge(main_free, G_KV + t + 1)
                act.activation(v_parts(v_h, t), kv[:, t, 256:512].rearrange("p (c x d) -> p c x d", c=2, x=2),
                               ACT.Copy).then_inc(vv_hi, 1)
                if t >= 2:
                    act.wait_ge(k_ss, t - 1)
                act.activation(kv_sq[:, t % 2, :], kv[:, t, 0:256], ACT.Square).then_inc(k_squared, 1)

            def q_part(j):
                act.wait_ge(chunk_used, C_Q + j + 1)
                act.activation(act_h[:, SLOT_Q + j, :], ps[:, B_Q + j % 2, :], ACT.Copy).then_inc(q_hi, 1)
                if j >= 2:
                    act.wait_ge(q_split, j)
                    act.activation(q_plain[:], ps[:, B_Q + j % 2, :], ACT.Copy).then_inc(q_copied, 1)
                if j >= 1:
                    act.wait_ge(q_summed, j)
                act.activation(q_sq[:], ps[:, B_Q + j % 2, :], ACT.Square).then_inc(q_squared, 1)

            def load_bias(c):
                heads = slice(8 * c, 8 * c + 8)
                act.dma_start(at_bias[:, heads, :],
                              bass.AP(lines.tensor, P - 1 + c * 8 * P * 384, [[383, P], [P * 384, 8], [1, 256]]))\
                    .then_inc(bias_landed[c], 16)

            tick(C_Q, 0)
            q_part(0)
            tick(C_Q + 1, 1)
            q_part(1)
            act.wait_ge(lines_stored, 16)
            act.wait_ge(vv_lo, TT)
            act.wait_ge(k_normed, TT)
            load_bias(0)
            for c in range(2):
                act.wait_ge(k_turned, 4 * c + 4)
                for x in range(2):
                    part = slice(x * HD, (x + 1) * HD)
                    act.activation(act_h[part, SLOT_K + 2 * c + x, :], ps[part, B_O + c, :], ACT.Copy)\
                        .then_inc(kt_hi, 1)
            load_bias(1)
            tick(C_Q + 2, 2)

            def attend(u):
                w = u - LAG_T
                if 0 <= w < UNITS:
                    first_half = 256 if unit(w)[1] == 0 else 0
                    act.wait_ge(p_turned, w + 1)
                    if w >= P_RING:
                        act.wait_ge(o_full, (w - P_RING) // 2 + 1)
                    act.activation(act_h[:, SLOT_P + w % P_RING, first_half:], ps[:, B_T + w % 2, first_half:],
                                   ACT.Copy).then_inc(p_hi, 1)
                if u < UNITS:
                    first_key = P if unit(u)[1] == 0 else 0
                    act.wait_ge(sink_off, u + 1)
                    for x in range(2):
                        s = at_s[:, u % S_RING, x, first_key:]
                        act.activation(s, s, ACT.Exp, bias=soft[:, 0, 2 * u + x:2 * u + x + 1],
                                       accum_out=soft[:, 2, 2 * u + x:2 * u + x + 1]).then_inc(p_exp, 1)
                    act.activation(soft[:, 3, 2 * u:2 * u + 2], soft[:, 1, 2 * u:2 * u + 2], ACT.Exp)\
                        .then_inc(sink_exp, 1)
                w = u - LAG_O
                if w % 4 == 3 and 0 <= w < UNITS:
                    act.wait_ge(o_full, w // 2 + 1)
                    act.activation(quad(act_h, w // 4), quad_bank(w // 4), ACT.Copy).then_inc(o_hi, 1)
                if u % 4 == 0 and u // 4 + 2 < KT:
                    q_part(u // 4 + 2)
                back = 1 if u < WO_STEP else 2
                if filler_chunk(u - back) is not None:
                    tick(filler_chunk(u - back), filler_chunk(u - back) % RING)

            for u in range(STEPS):
                attend(u)
            for j in range(KT // 2):
                tick(C_WO + 4 + j, j)
                for d in (2 * j, 2 * j + 1):
                    spread_hi(3, d, colp[:, PC_FFN + KT + d:PC_FFN + KT + d + 1], out_free, A_WO + d + 1, d == 0)
            ffn(1, C_UP1, G_UP1)
            project(4, C_DN1, A_DN1, 3, 0)

        @block.vector
        def _(dve):
            def tick(c, slot):
                if isinstance(c, int) and c + AHEAD >= CHUNKS:
                    return
                split(c + AHEAD, (slot + AHEAD) % RING)

            def split(c, slot):
                dve.wait_ge(hi_split, c + 1)
                dve.tensor_tensor(w_l[:, slot, :], raw[:, slot % RAW, :], w_h[:, slot, :].bitcast(F32),
                                  ALU.subtract).then_inc(lo_split, 1)

            def gain_lo(n, d, gain):
                dve.wait_ge(hn_hi, KT * n + d + 1)
                dve.scalar_tensor_tensor(out=hn_l[:, d, :], in0=h[:, d, :], scalar=gain,
                                         in1=hn_h[:, d, :].bitcast(F32), op0=ALU.mult, op1=ALU.subtract)\
                    .then_inc(hn_lo, 1)

            def add_squares(n, d, first, squares):
                dve.wait_ge(squared, KT * n + d + 1)
                if first:
                    dve.tensor_copy(sq_sum, squares).then_inc(sq_added, 1)
                else:
                    dve.wait_ge(sq_added, KT * n + d)
                    dve.tensor_tensor(sq_sum, sq_sum, squares, ALU.add).then_inc(sq_added, 1)

            def spread_lo(n, d, gain, first):
                gain_lo(n, d, gain)
                add_squares(n, d, first, sq)

            def finish_norm(n, c, row):
                tick(c, 0)
                dve.wait_ge(col_summed, n + 1)
                dve.tensor_scalar(mean[:, 0:TT], ps[:, MISC, 0:TT], 1.0 / D_MODEL, EPS, ALU.mult, ALU.add)\
                    .then_inc(mean_ready, 1)
                dve.wait_ge(r_ready, n + 1)
                if row is None:
                    return
                dve.tensor_tensor(diag, ident[:].unsqueeze(1).broadcast_to([P, TT, P]),
                                  r_col[:].unsqueeze(2).broadcast_to([P, TT, P]), ALU.mult)\
                    .then_inc(diag_ready, 1)
                tick(c + 1, 1)
                dve.wait_ge(row_spread, row + 1)
                dve.tensor_copy(r_row[:], ps[:, MISC, :]).then_inc(row_ready, 1)
                dve.wait_ge(row_ready, row + 1)

            def project(n, base, a_base, chunks, gain_col, banks=4):
                per = {3: 4, 2: 2, 1: 4}[chunks]

                def body(i, first, last):
                    for dd in range(per):
                        d = i * per + dd
                        for k in range(chunks):
                            tick(base + (i * per + dd) * chunks + k, (dd * chunks + k) % RING)
                        dve.wait_ge(chunk_used, base + (d + 1) * chunks)
                        dve.tensor_tensor(h[:, d, :], ps[:, banks + dd % 2, :], h[:, d, :], ALU.add)\
                            .then_inc(out_free, 1)
                        if n < 4:
                            dve.wait_ge(out_free, a_base + d + 1)
                            spread_lo(n, d, colp[:, bass.ds(gain_col + d, 1)], first and dd == 0)

                rolled(dve, KT // per, body)

            def ffn(layer, base, g_base):
                def product_lo(pair, pp, par):
                    dve.wait_ge(prod_hi, pair + 1)
                    dve.tensor_tensor(act_l[:, pp, :], ff_p[:, par, :], act_h[:, pp, :].bitcast(F32),
                                      ALU.subtract).then_inc(prod_lo, 1)

                def body(i, first, last):
                    for k in range(4):
                        tile = 4 * i + k
                        n = 44 * layer + tile
                        pair = PAIRS * layer + 2 * i + k // 2
                        pc = PC_CONV + 4 * (44 * layer + tile)
                        dve.wait_ge(chunk_used, base + tile + 1)
                        if not (first and layer == 0 and k < 2):
                            dve.wait_ge(conv_0, n - 1)
                        dve.tensor_tensor(ff_a[:, k % 2, 2:514], ps[:, k, :], r_row[:], ALU.mult)\
                            .then_inc(main_free, 1)
                        if k % 2 == 0 and not (first and k == 0):
                            product_lo(pair - 1, 2 * i + k // 2 - 1, (k // 2 + 1) % 2)
                        if not (first and k < 2):
                            tick(base + tile, k)
                        dve.wait_ge(conv_0, n + 1)
                        dve.scalar_tensor_tensor(out=ff_c[:, k, :], in0=ff_a[:, k % 2, 1:513],
                                                 scalar=colp[:, bass.ds(pc + 1, 1)], in1=ff_c[:, k, :],
                                                 op0=ALU.mult, op1=ALU.add).then_inc(conv_1, 1)
                        dve.wait_ge(conv_1, n + 1)
                        dve.scalar_tensor_tensor(out=ff_c[:, k, :], in0=ff_a[:, k % 2, 0:512],
                                                 scalar=colp[:, bass.ds(pc, 1)], in1=ff_c[:, k, :],
                                                 op0=ALU.mult, op1=ALU.add).then_inc(conv_2, 1)
                        if k % 2 == 1:
                            dve.wait_ge(silu_done, pair + 1)
                            dve.wait_ge(conv_2, n + 1)
                            dve.tensor_tensor(ff_p[:, k // 2, :], ff_c[:, k - 1, :], ff_c[:, k, :],
                                              ALU.mult).then_inc(prod, 1)

                finish_norm(2 * layer + 1, base, layer + 1)
                dve.memset(ff_a[:, :, 0:2], 0.0).then_inc(pads_zeroed, 1)
                dve.wait_ge(pads_zeroed, layer + 1)
                rolled(dve, PAIRS // 2, body)
                product_lo(PAIRS * (layer + 1) - 1, PAIRS - 1, 1)

            dve.memset(halves[:], 0.0).then_inc(halves_ready, 1)
            dve.wait_ge(halves_ready, 1)
            dve.memset(halves[0:HD, 0:1], 1.0).then_inc(halves_ready, 1)
            dve.memset(halves[HD:P, 1:2], 1.0).then_inc(halves_ready, 1)
            dve.wait_ge(params_landed, 16)
            for d in range(KT):
                if d % 3 == 0 and d // 3 < RAW:
                    split(d // 3, d // 3)
                dve.wait_ge(x_landed[d], 16)
                gain_lo(0, d, colp[:, PC_MIX + d:PC_MIX + d + 1])
            for d in range(KT):
                if d == 2:
                    split(2, 2)
                add_squares(0, d, d == 0, sq_start[d % 2])
            dve.wait_ge(rows_landed, 16)
            dve.tensor_scalar(negsink[:], rowp[:, PR_SINK:PR_ALL], -1.0, None, ALU.mult)\
                .then_inc(gains_ready, 1)
            dve.tensor_tensor(qk_gain[:], rowp[:, PR_QG:PR_QG + HD], rowp[:, PR_KG:PR_KG + HD], ALU.mult)\
                .then_inc(gains_ready, 1)
            dve.wait_ge(lines_summed, 1)
            dve.tensor_tensor(line_sb, ps[0:HEADS, 6, 0:384], masked_sb, ALU.add).then_inc(lines_ready, 1)
            finish_norm(0, C_V, 0)

            def v_lo_part(j, t):
                u = 4 * j + t
                dve.wait_ge(v_hi, u + 1)
                dve.tensor_tensor(act_l[:, bass.ds(4 * j, 4), t * P:(t + 1) * P],
                                  sg_u[:, t % 2, :].rearrange("p (g d) -> p g d", g=4),
                                  act_h[:, bass.ds(4 * j, 4), t * P:(t + 1) * P].bitcast(F32),
                                  ALU.subtract).then_inc(v_lo, 1)

            def v_block(j, first, last):
                for q in range(3):
                    if not (first and q < 2):
                        tick(C_V + 4 * j + q, q)
                for t in range(TT):
                    if t == 2 and not first:
                        tick(C_V + 4 * j + 3, 3)
                    u = 4 * j + t
                    if t < TT - 1:
                        dve.wait_ge(v_full, 3 * j + t + 1)
                    else:
                        dve.wait_ge(chunk_used, C_V + 4 * j + 4)
                    if not (first and t < 2):
                        dve.wait_ge(v_gelu, u - 1)
                    dve.tensor_scalar(sg_a[:, t % 2, :], ps[:, t, :], r_col[:, t:t + 1], None, ALU.mult)\
                        .then_inc(main_free, 1)
                    if t >= 1:
                        v_lo_part(j, t - 1)
                if first:
                    tick(C_V + 4 * j + 3, 3)
                v_lo_part(j, TT - 1)

            rolled(dve, 4, v_block)

            dve.wait_ge(v_squared, 4 * TT)
            dve.tensor_reduce(mean[:, 8:8 + TT], v_sq[:], AX_X, ALU.add).then_inc(v_sum, 1)
            dve.wait_ge(v_sum, 1)
            dve.tensor_scalar(mean[:, 0:TT], mean[:, 8:8 + TT], 1.0 / (GROUPS * P), EPS, ALU.mult, ALU.add)\
                .then_inc(vmean_ready, 1)

            def wr_part(g, par):
                dve.wait_ge(wr_hi, g + 1)
                dve.tensor_tensor(act_h[:, SLOT_W + 2 + par, :], sg_w[:, par, :],
                                  act_h[:, SLOT_W + par, :].bitcast(F32),
                                  ALU.subtract).then_inc(wr_lo, 1)

            def spread_sums(par):
                return ps[:, 4 + 2 * par:6 + 2 * par, :].rearrange("p k (c z t) -> p z (k c) t", c=2, z=2)

            def mix_hi(g, par, slot, turn):
                dve.wait_ge(mix_full, g + 1)
                dve.wait_ge(b_landed[slot], 16 * (turn + 1))
                if not (isinstance(g, int) and g < 2):
                    dve.wait_ge(gated_lo, g - 1)
                dve.scalar_tensor_tensor(out=sg_s[par].rearrange("p (c t) -> p c t", c=TT),
                                         in0=spread_sums(par)[:, 0], scalar=colp[:, bass.ds(PC_VG + g, 1)],
                                         in1=ring_b[:, slot, :].unsqueeze(1).broadcast_to([P, TT, P]),
                                         op0=ALU.mult, op1=ALU.add).then_inc(mixed, 1)

            def mix_lo(g, par):
                dve.wait_ge(mixed, g + 1)
                s = sg_s[par].rearrange("p (c t) -> p c t", c=TT)
                dve.scalar_tensor_tensor(out=s, in0=spread_sums(par)[:, 1], scalar=colp[:, bass.ds(PC_VG + g, 1)],
                                         in1=s, op0=ALU.mult, op1=ALU.add).then_inc(out_free, 1)

            def gate(g, par):
                dve.wait_ge(out_free, A_S + g + 1)
                dve.wait_ge(u_gelu, g + 1)
                dve.tensor_tensor(sg_s[par], sg_s[par], sg_u[:, par, :], ALU.mult).then_inc(gated, 1)

            def gate_lo(g, par):
                dve.wait_ge(gated_hi, g + 1)
                dve.tensor_tensor(act_l[:, g, :], sg_s[par], act_h[:, g, :].bitcast(F32), ALU.subtract)\
                    .then_inc(gated_lo, 1)

            wr_part(0, 0)

            def u_block(i, first, last):
                for k in range(4):
                    g = 4 * i + k
                    dve.wait_ge(chunk_used, C_U + g + 1)
                    if not (first and k < 2):
                        dve.wait_ge(u_gelu, g - 1)
                    dve.tensor_tensor(sg_a[:, k % 2, :], ps[:, k, :], r_row[:], ALU.mult).then_inc(main_free, 1)
                    if not (first and k < 2):
                        gate_lo(g - 2, k % 2)
                    if not (first and k == 0):
                        mix_hi(g - 1, (k + 1) % 2, (k + 3) % 4, i - 1 if k == 0 else i)
                    if not (last and k == 3):
                        wr_part(g + 1, (k + 1) % 2)
                    if not (first and k == 0):
                        mix_lo(g - 1, (k + 1) % 2)
                    if not (last and k == 3):
                        tick(C_U + g, k)
                    if not (first and k == 0):
                        gate(g - 1, (k + 1) % 2)

            rolled(dve, GROUPS // 4, u_block)
            gate_lo(GROUPS - 2, 0)
            mix_hi(GROUPS - 1, 1, 3, 3)
            mix_lo(GROUPS - 1, 1)
            gate(GROUPS - 1, 1)
            gate_lo(GROUPS - 1, 1)
            tick(C_U + GROUPS - 1, 3)
            project(1, C_OUT, A_OUT, 2, PC_FFN, 0)
            ffn(0, C_UP0, G_UP0)
            project(2, C_DN0, A_DN0, 3, PC_MIX + KT)

            def q_lo(j):
                dve.wait_ge(q_squared, j + 1)
                dve.tensor_tensor(act_l[:, SLOT_Q + j, :], ps[:, B_Q + j % 2, :],
                                  act_h[:, SLOT_Q + j, :].bitcast(F32), ALU.subtract).then_inc(q_split, 1)

            def q_means(j):
                part = slice(8 * j, 8 * j + 8)
                two = lambda x: x.rearrange("p (t x) -> p t x", t=TT)
                dve.wait_ge(q_summed, j + 1)
                dve.wait_ge(rx_ready, 2)
                dve.tensor_tensor(two(r_q[:, part]), two(ps[:, B_Q + j % 2, 0:8]),
                                  r2_col[:].unsqueeze(2).broadcast_to([P, TT, 2]), ALU.mult).then_inc(q_scaled, 1)
                dve.wait_ge(q_scaled, j + 1)
                dve.tensor_scalar(mean[:, part], r_q[:, part], 1.0 / HD, EPS, ALU.mult, ALU.add)\
                    .then_inc(q_mean, 1)

            finish_norm(2, C_KV, None)
            dve.tensor_tensor(r2_col[:], r_col[:], r_col[:], ALU.mult).then_inc(rx_ready, 1)
            dve.tensor_scalar(r8_col[:], r_col[:], HD ** -0.5, None, ALU.mult).then_inc(rx_ready, 1)
            for q in range(1, 4):
                tick(C_KV + q, q)
            for t in range(TT):
                if t < TT - 1:
                    dve.wait_ge(kv_full, t + 1)
                else:
                    dve.wait_ge(chunk_used, C_KV + 4)
                dve.tensor_scalar(kv[:, t, :], ps[:, t, :], r_col[:, t:t + 1], None, ALU.mult)\
                    .then_inc(main_free, 1)
                dve.wait_ge(k_squared, t + 1)
                dve.tensor_reduce(mean[:, 32 + 4 * t:36 + 4 * t],
                                  kv_sq[:, t % 2, :].rearrange("p (g d) -> p g d", g=KV_HEADS), AX_X, ALU.add)\
                    .then_inc(k_ss, 1)
            dve.wait_ge(k_ss, TT)
            dve.tensor_scalar(mean[:, 0:16], mean[:, 32:48], 1.0 / HD, EPS, ALU.mult, ALU.add)\
                .then_inc(k_mean, 1)
            for t in range(TT):
                dve.wait_ge(vv_hi, t + 1)
                dve.tensor_tensor(v_parts(v_l, t), kv[:, t, 256:512].rearrange("p (c x d) -> p c x d", c=2, x=2),
                                  v_parts(v_h, t).bitcast(F32), ALU.subtract).then_inc(vv_lo, 1)
            tick(C_Q, 0)
            q_lo(0)
            dve.wait_ge(rk_ready, 1)
            dve.wait_ge(gains_ready, 2)
            for t in range(TT):
                k_view = kv[:, t, 0:256].rearrange("p (g d) -> p g d", g=KV_HEADS)
                n_view = k_n[:, t, :].rearrange("p (g d) -> p g d", g=KV_HEADS)
                dve.tensor_tensor(k_view, k_view, r_k[:, 4 * t:4 * t + 4].unsqueeze(2)
                                  .broadcast_to([P, KV_HEADS, HD]), ALU.mult).then_inc(k_scaled, 1)
                if t == 1:
                    q_means(0)
                dve.wait_ge(k_scaled, t + 1)
                dve.tensor_tensor(n_view, k_view, qk_gain[:].unsqueeze(1).broadcast_to([P, KV_HEADS, HD]),
                                  ALU.mult).then_inc(k_normed, 1)

            def q_factors(j):
                part = slice(8 * j, 8 * j + 8)
                two = lambda x: x.rearrange("p (t x) -> p t x", t=TT)
                dve.wait_ge(q_pow, j + 1)
                dve.tensor_tensor(two(r_q[:, part]), two(r_q[:, part]),
                                  r8_col[:].unsqueeze(2).broadcast_to([P, TT, 2]), ALU.mult).then_inc(rq_ready, 1)

            tick(C_Q + 1, 1)
            q_lo(1)
            for c in range(2):
                for x in range(2):
                    part = slice(x * HD, (x + 1) * HD)
                    dve.wait_ge(kt_hi, 2 * c + x + 1)
                    dve.tensor_tensor(act_l[part, SLOT_K + 2 * c + x, :], ps[part, B_O + c, :],
                                      act_h[part, SLOT_K + 2 * c + x, :].bitcast(F32), ALU.subtract)\
                        .then_inc(kt_lo, 1)
            q_means(1)
            q_factors(0)
            tick(C_Q + 2, 2)

            def attend(u):
                if u % 4 == 3 and u // 4 + 2 < KT:
                    q_means(u // 4 + 2)
                if u % 4 == 1 and u // 4 + 1 < KT:
                    q_factors(u // 4 + 1)
                late = u - WO_STEP - 1
                if late >= 0 and late % 2 == 1:
                    d = late // 2
                    if d % 2:
                        dve.wait_ge(chunk_used, C_WO + d // 2 + 1)
                    else:
                        dve.wait_ge(wo_half, d // 2 + 1)
                    dve.tensor_tensor(h[:, d, :], ps[:, B_Q + d % 2, :], h[:, d, :], ALU.add)\
                        .then_inc(wo_added, 1)
                if u < UNITS:
                    j, n = unit(u)
                    first_key = P if n == 0 else 0
                    if n == 0:
                        dve.wait_ge(rq_ready, j + 1)
                        dve.wait_ge(bias_landed[j // 4], 16)
                    dve.wait_ge(s_full, u + 1)
                    if u >= S_RING:
                        dve.wait_ge(p_turned, u - S_RING + 1)
                    col = 8 * j + 2 * n
                    for x in range(2):
                        dve.scalar_tensor_tensor(out=at_s[:, u % S_RING, x, first_key:],
                                                 in0=ps[:, B_S + u % 2, x * 256 + first_key:(x + 1) * 256],
                                                 scalar=r_q[:, col + x:col + x + 1],
                                                 in1=at_bias[:, 2 * j + x, first_key:],
                                                 op0=ALU.mult, op1=ALU.add).then_inc(s_biased, 1)
                    dve.wait_ge(s_biased, 2 * u + 2)
                    two = slice(2 * u, 2 * u + 2)
                    dve.tensor_reduce(soft[:, 4, two], at_s[:, u % S_RING, :, first_key:], AX_X, ALU.max)\
                        .then_inc(s_max, 1)
                if 1 <= u < UNITS + 1:
                    w = u - 1
                    last = slice(2 * w, 2 * w + 2)
                    dve.wait_ge(sink_exp, w + 1)
                    dve.tensor_tensor(soft[:, 4, last], soft[:, 2, last], soft[:, 3, last], ALU.add).then_inc(den, 1)
                if u < UNITS:
                    dve.wait_ge(s_max, u + 1)
                    dve.scalar_tensor_tensor(out=soft[:, 0, two], in0=soft[:, 4, two], scalar=-1.0,
                                             in1=negsink[:, 2 * j:2 * j + 2], op0=ALU.mult, op1=ALU.min)\
                        .then_inc(m_ready, 1)
                if 1 <= u < UNITS + 1:
                    dve.wait_ge(den, w + 1)
                    dve.reciprocal(soft[:, 5, last], soft[:, 4, last]).then_inc(rden, 1)
                if u < UNITS:
                    dve.wait_ge(m_ready, u + 1)
                    dve.tensor_tensor(soft[:, 1, two], soft[:, 0, two],
                                      rowp[:, PR_SINK + 2 * j:PR_SINK + 2 * j + 2], ALU.add).then_inc(sink_off, 1)
                w = u - LAG_T
                if 0 <= w < UNITS:
                    first_half = 256 if unit(w)[1] == 0 else 0
                    dve.wait_ge(p_hi, w + 1)
                    dve.tensor_tensor(act_l[:, SLOT_P + w % P_RING, first_half:], ps[:, B_T + w % 2, first_half:],
                                      act_h[:, SLOT_P + w % P_RING, first_half:].bitcast(F32), ALU.subtract)\
                        .then_inc(p_lo, 1)
                w = u - LAG_O
                if w % 4 == 3 and 0 <= w < UNITS:
                    dve.wait_ge(o_hi, w // 4 + 1)
                    dve.tensor_tensor(quad(act_l, w // 4), quad_bank(w // 4), quad(act_h, w // 4).bitcast(F32),
                                      ALU.subtract).then_inc(o_lo, 1)

            for u in range(STEPS + 1):
                attend(u)
            dve.wait_ge(lo_split, C_WO + 4 + AHEAD)
            dve.wait_ge(wo_added, KT)
            for d in range(KT + 1):
                if d < KT:
                    if d % 2 == 0:
                        dve.wait_ge(wo_even_full, d // 2 + 1)
                    else:
                        dve.wait_ge(chunk_used, C_WO + 4 + d // 2 + 1)
                    dve.tensor_tensor(h[:, d, :], ps[:, 4 + d % 2, :], h[:, d, :], ALU.add).then_inc(out_free, 1)
                if d >= 1:
                    gain_lo(3, d - 1, colp[:, PC_FFN + KT + d - 1:PC_FFN + KT + d])
                if d % 2 == 0 and d < KT:
                    tick(C_WO + 4 + d // 2, d // 2)
            ffn(1, C_UP1, G_UP1)
            project(4, C_DN1, A_DN1, 3, 0)

        @block.tensor
        def _(pe):
            def mm3(dst, stat_h, stat_l, mov_h, mov_l, start, stop):
                pe.matmul(dst, stat_h, mov_h, start=start, stop=False)
                pe.matmul(dst, stat_h, mov_l, start=False, stop=False)
                return pe.matmul(dst, stat_l, mov_h, start=False, stop=stop)

            def norm_sums(n):
                pe.wait_ge(sq_added, KT * (n + 1))
                for t in range(TT):
                    m = pe.matmul(ps[:, MISC, t:t + 1], sq_sum[:, t * P:(t + 1) * P], ones[:, 0:1],
                                  start=True, stop=True)
                m.then_inc(col_summed, 1)

            def norm_row(row):
                pe.wait_ge(diag_ready, row + 1)
                pe.matmul(ps[:, MISC, :], ones[:], sq, start=True, stop=True).then_inc(row_spread, 1)

            def tile_chunk(c, slot, bank, n, wait_tiles):
                pe.wait_ge(lo_split, c + 1)
                for k in range(KT):
                    if wait_tiles:
                        pe.wait_ge(hn_lo, KT * n + k + 1)
                    b = operand_blocks(k)
                    m = mm3(ps[:, bank, :], w_h[:, slot, b], w_l[:, slot, b], hn_h[:, k, :], hn_l[:, k, :],
                            k == 0, k == KT - 1)
                m.then_inc(chunk_used, 1)

            def token_chunk(c, q, full, wait_bank, wait_tiles, n, between=None):
                pe.wait_ge(lo_split, c + 1)
                for t in range(TT):
                    if wait_bank is not None and q == 0:
                        pe.wait_ge(main_free, wait_bank + t)
                    for kk in range(2):
                        k = 2 * q + kk
                        if wait_tiles and t == 0:
                            pe.wait_ge(hn_lo, KT * n + k + 1)
                        rows_ = slice(t * P, (t + 1) * P)
                        cols_ = slice(kk * 512, (kk + 1) * 512)
                        start, stop = k == 0, k == KT - 1
                        pe.matmul(ps[:, t, :], hn_h[:, k, rows_], w_h[:, q, cols_], start=start, stop=False)
                        pe.matmul(ps[:, t, :], hn_h[:, k, rows_], w_l[:, q, cols_], start=False, stop=False)
                        m = pe.matmul(ps[:, t, :], hn_l[:, k, rows_], w_h[:, q, cols_], start=False, stop=stop)
                    if t == TT - 1:
                        m.then_inc(chunk_used, 1)
                    elif q == 3:
                        m.then_inc(full, 1)
                    if between is not None:
                        between(t)

            def project(base, a_base, chunks, tiles, ready, r_base, banks=4, last_use=None):
                per = {3: 4, 2: 2, 1: 4}[chunks]

                def body(i, first, last):
                    for dd in range(per):
                        d = i * per + dd
                        a = a_base + d
                        if last_use is not None and first and dd < 2:
                            pe.wait_ge(last_use[0], last_use[1] + dd)
                        else:
                            pe.wait_ge(out_free, a - 1)
                        for part in range(chunks):
                            c = base + (i * per + dd) * chunks + part
                            slot = (dd * chunks + part) % RING
                            pe.wait_ge(lo_split, c + 1)
                            for k in range(8 * part, min(8 * part + 8, tiles)):
                                if first and dd == 0:
                                    pe.wait_ge(ready, r_base + k + 1)
                                b = operand_blocks(k % 8)
                                m = mm3(ps[:, banks + dd % 2, :], w_h[:, slot, b], w_l[:, slot, b],
                                        act_h[:, k, :], act_l[:, k, :],
                                        k == 0, k == tiles - 1)
                            m.then_inc(chunk_used, 1)

                rolled(pe, KT // per, body)

            def ffn_up(n, base, g_base):
                def body(i, first, last):
                    for k in range(4):
                        if n == 1 and first and k < 2:
                            pe.wait_ge(out_free, A_OUT + KT - 1 + k)
                        else:
                            pe.wait_ge(main_free, g_base + 4 * i + k - 3)
                        tile_chunk(base + 4 * i + k, k, k, n, first and k == 0)
                        if first and k == 0:
                            norm_sums(n)
                        if first and k == 1:
                            norm_row((n + 1) // 2)

                rolled(pe, PAIRS // 2, body)

            pe.wait_ge(consts_ready, 1)
            for i in range(WARM_UP):
                m = pe.matmul(ps[:, MISC, 0:P], ones[:], ones[:], start=True, stop=True)
            m.then_inc(warmed, 1)

            token_chunk(C_V, 0, v_full, None, True, 0)
            pe.wait_ge(rel_landed, 16 * 3)
            pe.matmul(ps[0:HEADS, 6, 0:384], rel_sb, onehot_sb, start=True, stop=True)\
                .then_inc(lines_summed, 1)
            pe.wait_ge(consts_ready, 3)
            token_chunk(C_V + 1, 1, v_full, None, True, 0)
            token_chunk(C_V + 2, 2, v_full, None, True, 0, lambda t: norm_sums(0) if t == 1 else None)
            token_chunk(C_V + 3, 3, v_full, None, True, 0, lambda t: norm_row(0) if t == 0 else None)
            with pe.Fori(1, 4) as j:
                for q in range(4):
                    token_chunk(C_V + 4 * j + q, q, v_full, G_V + 4 * j - 3, False, 0)

            def spatial(g):
                pe.wait_ge(wr_lo, g + 1)
                if g >= 2:
                    pe.wait_ge(out_free, A_S + g - 1)
                for c in range(TT):
                    t = slice(c * P, (c + 1) * P)
                    w = SLOT_W + g % 2
                    both = ps[:, 4 + g % 2 * 2 + c // 2, c % 2 * 256:c % 2 * 256 + 256]
                    pe.matmul(both, act_h[:, g, t], act_h[:, w:w + 3:2, t], start=True, stop=False)
                    m = pe.matmul(both[:, 0:P], act_l[:, g, t], act_h[:, w, t], start=False, stop=True)
                m.then_inc(mix_full, 1)

            for g in range(GROUPS):
                pe.wait_ge(main_free, G_U + g - 3)
                tile_chunk(C_U + g, g % 4, g % 4, 0, False)
                if g == 1:
                    pe.wait_ge(v_lo, 16)
                if g >= 1:
                    spatial(g - 1)
            spatial(GROUPS - 1)
            project(C_OUT, A_OUT, 2, GROUPS, gated_lo, 0, 0, (main_free, G_U + GROUPS - 3))
            ffn_up(1, C_UP0, G_UP0)
            project(C_DN0, A_DN0, 3, PAIRS, prod_lo, 0)

            for q in range(4):
                token_chunk(C_KV + q, q, kv_full, G_KV - 3, True, 2)
                if q == 0:
                    norm_sums(2)

            def q_sums(j):
                pe.wait_ge(q_squared, j + 1)
                if j < 2:
                    pe.wait_ge(q_split, j + 1)
                else:
                    pe.wait_ge(q_copied, j - 1)
                for t in range(TT):
                    m = pe.matmul(ps[:, B_Q + j % 2, 2 * t:2 * t + 2], q_sq[:, t * P:(t + 1) * P],
                                  halves[:], start=True, stop=True)
                m.then_inc(q_summed, 1)

            def q_quarter(j, q):
                c = C_Q + j
                if q == 0:
                    pe.wait_ge(lo_split, c + 1)
                    if j == 1:
                        pe.wait_ge(mean_ready, 3)
                    elif j >= 2:
                        pe.wait_ge(q_scaled, j - 1)
                for k in (2 * q, 2 * q + 1):
                    b = operand_blocks(k)
                    m = mm3(ps[:, B_Q + j % 2, :], w_h[:, c % RING, b], w_l[:, c % RING, b], hn_h[:, k, :],
                            hn_l[:, k, :], k == 0, k == KT - 1)
                if q == 3:
                    m.then_inc(chunk_used, 1)

            def wo_quarter(w):
                c, d = C_WO + w // 4, w // 2
                if w == 0:
                    pe.wait_ge(o_lo, 4)
                if w in (0, 2):
                    pe.wait_ge(q_scaled, KT - 1 + w // 2)
                if w % 4 == 0:
                    pe.wait_ge(lo_split, c + 1)
                if w % 2 == 0 and d >= 2:
                    pe.wait_ge(wo_added, d - 1)
                for k in (2 * (w % 2), 2 * (w % 2) + 1):
                    b = operand_blocks(4 * (d % 2) + k)
                    m = mm3(ps[:, B_Q + d % 2, :], w_h[:, c % RING, b], w_l[:, c % RING, b], act_h[:, k, :],
                            act_l[:, k, :], k == 0, k == 3)
                if w % 2 == 1:
                    m.then_inc(chunk_used if d % 2 else wo_half, 1)

            def turn_k(c):
                for t in range(TT):
                    pe.wait_ge(k_normed, t + 1)
                    pe.transpose(ps[:, B_O + c, t * P:(t + 1) * P], k_n[:, t, c * P:(c + 1) * P], ident[:])\
                        .then_inc(k_turned, 1)

            pe.wait_ge(halves_ready, 3)
            for q in range(4):
                q_quarter(0, q)
            for q in range(4):
                q_quarter(1, q)
                if q == 2:
                    q_sums(0)
            q_quarter(2, 0)
            q_quarter(2, 1)
            pe.wait_ge(out_free, A_DN0 + KT)
            turn_k(0)
            turn_k(1)
            q_quarter(2, 2)
            q_sums(1)
            q_quarter(2, 3)

            def attend(u):
                if u % 4 == 3 and u // 4 + 2 < KT:
                    q_sums(u // 4 + 2)
                w = u - LAG_T
                if 0 <= w < UNITS:
                    pe.wait_ge(p_scaled, 2 * w + 2)
                    if w >= 2:
                        pe.wait_ge(p_lo, w - 1)
                    for half in range(1 if unit(w)[1] == 0 else 0, 2):
                        for x in range(2):
                            m = pe.transpose(ps[:, B_T + w % 2, (2 * half + x) * P:(2 * half + x + 1) * P],
                                             at_s[:, w % S_RING, x, half * P:(half + 1) * P], ident[:])
                    m.then_inc(p_turned, 1)
                if u < UNITS:
                    j, n = unit(u)
                    if u == 0:
                        pe.wait_ge(kt_lo, 4)
                        pe.wait_ge(padded, 4)
                    if n == 0:
                        pe.wait_ge(q_split, j + 1)
                    if u >= 2:
                        pe.wait_ge(s_biased, 2 * u - 2)
                    first_key = P if n == 0 else 0
                    keys = slice((n - 1) * P + first_key, (n + 1) * P)
                    q = slice(n * P, (n + 1) * P)
                    k_slot = SLOT_K + 2 * (j // 4)
                    mm3(ps[:, B_S + u % 2, :].rearrange("p (x k) -> p x k", x=2)[:, :, first_key:],
                        act_h[:, j, q], act_l[:, j, q], act_h[:, k_slot:k_slot + 2, keys],
                        act_l[:, k_slot:k_slot + 2, keys], True, True).then_inc(s_full, 1)
                w = u - LAG_PV
                if w % 2 == 1 and 0 <= w < UNITS:
                    j, n = unit(w)
                    if w % 4 == 1 and w >= 8:
                        pe.wait_ge(o_lo, w // 4 - 1)
                    pe.wait_ge(p_lo, w + 1)
                    if w == 1:
                        pe.wait_ge(vv_lo, TT)
                    slot = SLOT_P + (w - 1) % P_RING
                    terms = [(half, x) for half in ([1] if n == 0 else [0, 1]) for x in range(2)]
                    for half, x in terms:
                        v = (n - 1 + half) * 384 + j // 4 * 192 + x * HD
                        pt = slice(half * 256 + x * P, half * 256 + (x + 1) * P)
                        m = mm3(ps[:, B_O + w // 4 % 2, n % 2 * 256:n % 2 * 256 + 256], v_h[:, v:v + P],
                                v_l[:, v:v + P], act_h[:, slot:slot + 2, pt], act_l[:, slot:slot + 2, pt],
                                (half, x) == terms[0], (half, x) == terms[-1])
                    m.then_inc(o_full, 1)
                if u < 4 * (KT - Q_EARLY):
                    q_quarter(u // 4 + Q_EARLY, u % 4)
                elif u >= WO_STEP:
                    wo_quarter(u - WO_STEP)

            for u in range(STEPS):
                attend(u)
            for j in range(KT // 2):
                c = C_WO + 4 + j
                pe.wait_ge(lo_split, c + 1)
                for d in (2 * j, 2 * j + 1):
                    if d >= 2:
                        pe.wait_ge(out_free, A_WO + d - 1)
                    for k in range(4):
                        if d == 0:
                            pe.wait_ge(o_lo, KT)
                        b = operand_blocks(4 * (d % 2) + k)
                        m = mm3(ps[:, 4 + d % 2, :], w_h[:, j, b], w_l[:, j, b], act_h[:, 4 + k, :],
                                act_l[:, 4 + k, :], k == 0, k == 3)
                    m.then_inc(wo_even_full if d % 2 == 0 else chunk_used, 1)
            ffn_up(3, C_UP1, G_UP1)
            project(C_DN1, A_DN1, 3, PAIRS, prod_lo, PAIRS)


def bucket_of_distance():
    n = np.arange(MAX_DIST)
    exact = BUCKETS // 2
    large = exact + (np.log(np.maximum(n, 1).astype(np.float32) / exact)
                     / math.log(MAX_DIST / exact) * (BUCKETS - exact)).astype(np.int32)
    return np.where(n < exact, n, np.minimum(large, BUCKETS - 1))


def constants():
    onehot = np.zeros((BUCKETS, 384), np.float32)
    masked = np.full((HEADS, 384), MASKED, np.float32)
    for dist, b in enumerate(bucket_of_distance()):
        onehot[b, 255 - dist] = 1.0
        masked[:, 255 - dist] = 0.0
    return onehot, masked


def kernel(**inputs):
    import concourse.bacc as bacc
    from concourse.bass_utils import run_bass_kernel_spmd

    a = {k: np.asarray(v) for k, v in inputs.items()}

    def by_tile(w):
        k, n = w.shape
        blocks = w.reshape(k // P, P, n // P, P).transpose(2, 1, 0, 3)
        parts = []
        for tile in blocks:
            for lo in range(0, k // P, 8):
                part = tile[:, lo:lo + 8].reshape(P, -1)
                parts.append(np.pad(part, ((0, 0), (0, CHUNK - part.shape[1]))))
        return np.stack(parts)

    def by_token(w):
        n = w.shape[1]
        return w.reshape(4, 2, P, n // 512, 512).transpose(3, 0, 2, 1, 4).reshape(-1, P, CHUNK)

    def by_halves(w):
        return w.reshape(2, 4, P, 4, 2, P).transpose(0, 3, 2, 4, 1, 5).reshape(-1, P, CHUNK)

    def pairs(w, axis):
        w = np.moveaxis(w, axis, -1)
        w = w.reshape(w.shape[:-1] + (2, PAIRS, P))
        w = np.swapaxes(w, -3, -2)
        return np.moveaxis(w.reshape(w.shape[:-3] + (2 * PAIRS * P,)), -1, axis)

    heads = np.arange(HEADS).reshape(2, 2, 4).transpose(0, 2, 1).reshape(-1)
    w_in = a["sgu_w_in"][0]
    w_qkv = a["attn_w_qkv"][0]
    w_q = w_qkv[:, :D_MODEL].reshape(D_MODEL, HEADS, HD)[:, heads].reshape(D_MODEL, D_MODEL)
    w_o = a["attn_w_o"][0].reshape(HEADS, HD, D_MODEL)[heads].reshape(D_MODEL, D_MODEL)
    stream = np.concatenate([
        by_token(w_in[:, 2 * D_MODEL:]), by_tile(w_in[:, :2 * D_MODEL]), by_tile(a["sgu_w_out"][0]),
        by_tile(pairs(a["ffn_w_up"][0], 1)), by_tile(a["ffn_w_down"][0]),
        by_token(w_qkv[:, D_MODEL:]), by_tile(w_q), by_halves(w_o),
        by_tile(pairs(a["ffn_w_up"][1], 1)), by_tile(a["ffn_w_down"][1])])
    down = lambda v: v.reshape(-1, P).T
    conv = [np.stack([*pairs(a["ffn_conv_w"][i], 1), pairs(a["ffn_conv_b"][i], 0)], -1)
            .reshape(2 * PAIRS, P, 4).transpose(1, 0, 2).reshape(P, -1) for i in range(2)]
    cols = np.concatenate([down(a["mix_norm"]), down(a["ffn_norm"]), down(a["sgu_v_gain"][0]), *conv], 1)
    rows = np.concatenate([a["attn_q_gain"][0], a["attn_k_gain"][0], a["attn_sinks"][0][heads]])
    onehot, masked = constants()
    arrays = {
        "x_t": a["x"][0].T.reshape(KT, P, SEQ),
        "stream": stream,
        "cols": cols,
        "rows": rows,
        "ws_t": a["sgu_w_s"][0].transpose(0, 2, 1),
        "b_s": a["sgu_b_s"][0],
        "rel": a["rel_bias"][:, heads],
        "onehot": onehot,
        "masked": masked,
    }
    arrays = {k: np.ascontiguousarray(v) for k, v in arrays.items()}
    nc = bacc.Bacc("TRN2", target_bir_lowering=False, num_devices=1)
    args = [nc.dram_tensor(k, v.shape, F32, kind="ExternalInput").ap() for k, v in arrays.items()]
    args.append(nc.dram_tensor("out_t", (KT, P, SEQ), F32, kind="ExternalOutput").ap())
    build(nc, *args)
    r = run_bass_kernel_spmd(nc, [arrays], core_ids=[0])
    return np.ascontiguousarray(r.results[0]["out_t"].reshape(D_MODEL, SEQ).T)[None]
```
